# Optimizing a Trainium2 kernel written in Bass

```python
import math
import jax, jax.numpy as jnp
from jax import lax
import numpy as np

D_MODEL = 1024
BATCH = 1
SEQ = 256
DEPTH = 2

CHUNK = 64
N_PREV_CHUNKS = 8
BAND = CHUNK * (N_PREV_CHUNKS + 1)
MAX_REL = 128
HEAD_DIM = 64
MIX_WIDTH = D_MODEL
D_SB = MIX_WIDTH // 2
D_CA = MIX_WIDTH - D_SB
H_SB = D_SB // HEAD_DIM
H_CA = D_CA // HEAD_DIM
SB_QBLOCK = 128
D_FF = int(round(8 * D_MODEL / 3 / 256)) * 256
FFN_RESIDUAL = 0.5
ALPHA = (2 * DEPTH) ** 0.25
BETA_INIT = (8 * DEPTH) ** -0.25
LN_EPS = 1e-5
RMS_EPS = 1e-6

kernel_name = "hybrid_stickbreak_chunkattn_macaron_deepnorm"

def layer_norm(x, g, b):
    xf = x.astype(jnp.float32)
    mu = jnp.mean(xf, axis=-1, keepdims=True)
    xc = xf - mu
    var = jnp.mean(xc * xc, axis=-1, keepdims=True)
    y = xc * lax.rsqrt(var + LN_EPS) * g.astype(jnp.float32) + b.astype(jnp.float32)
    return y.astype(x.dtype)

def swiglu(x, w_gate, w_up, w_down):
    return (jax.nn.silu(x @ w_gate) * (x @ w_up)) @ w_down

def head_rmsnorm(o, g):
    of = o.astype(jnp.float32)
    of = of * lax.rsqrt(jnp.mean(of * of, axis=-1, keepdims=True) + RMS_EPS)
    b, s, h, d = o.shape
    return (of.reshape(b, s, h * d) * g.astype(jnp.float32)).astype(o.dtype)

def stick_breaking_attention(q, k, v):
    seq = q.shape[2]
    scale = 1.0 / math.sqrt(q.shape[-1])
    outs = []
    for i in range(seq // SB_QBLOCK):
        q0 = i * SB_QBLOCK
        q1 = q0 + SB_QBLOCK
        qi = q[:, :, q0:q1]
        kp = k[:, :, :q1]
        vp = v[:, :, :q1]
        z = jnp.einsum('bhqd,bhkd->bhqk', qi, kp).astype(jnp.float32) * scale
        t_pos = q0 + jnp.arange(SB_QBLOCK)[:, None]
        s_pos = jnp.arange(q1)[None, :]
        causal = s_pos < t_pos
        log_keep = jnp.where(causal, jax.nn.log_sigmoid(-z), 0.0)
        log_surv = lax.cumsum(log_keep, axis=3, reverse=True) - log_keep
        w = jnp.where(causal, jnp.exp(jax.nn.log_sigmoid(z) + log_surv), 0.0)
        outs.append(jnp.einsum('bhqk,bhkd->bhqd', w.astype(v.dtype), vp))
    return jnp.concatenate(outs, axis=2)

def chunked_rel_attention(q, k, v, rel_bias):
    b, seq, h, d = q.shape
    n_chunks = seq // CHUNK
    pad = N_PREV_CHUNKS * CHUNK
    scale = 1.0 / math.sqrt(d)
    k_pad = jnp.pad(k, ((0, 0), (pad, 0), (0, 0), (0, 0)))
    v_pad = jnp.pad(v, ((0, 0), (pad, 0), (0, 0), (0, 0)))
    qi = jnp.arange(CHUNK)[:, None]
    kj = jnp.arange(BAND)[None, :]
    rel = qi + pad - kj
    bias = rel_bias[:, jnp.clip(rel, -MAX_REL, MAX_REL) + MAX_REL].astype(jnp.float32)
    neg = jnp.finfo(jnp.float32).min

    def one_chunk(c):
        start = c * CHUNK
        qc = lax.dynamic_slice_in_dim(q, start, CHUNK, axis=1)
        kc = lax.dynamic_slice_in_dim(k_pad, start, BAND, axis=1)
        vc = lax.dynamic_slice_in_dim(v_pad, start, BAND, axis=1)
        sc = jnp.einsum('bqhd,bkhd->bhqk', qc, kc).astype(jnp.float32) * scale + bias
        valid = (start - pad + jnp.arange(BAND)) >= 0
        sc = jnp.where(valid[None, None, None, :], sc, neg)
        p = jax.nn.softmax(sc, axis=-1).astype(v.dtype)
        return jnp.einsum('bhqk,bkhd->bqhd', p, vc)

    out = lax.map(one_chunk, jnp.arange(n_chunks))
    return jnp.moveaxis(out, 0, 1).reshape(b, seq, h, d)

def setup_inputs(seed: int = 0) -> dict:
    key = jax.random.key(seed)
    ks = jax.random.split(key, 32)
    f32 = jnp.float32
    L, D, F = DEPTH, D_MODEL, D_FF
    std_d = D ** -0.5
    std_f = F ** -0.5

    def nrm(k, shape, std):
        return jax.random.normal(k, shape, f32) * std

    def gain(k, shape):
        return 1.0 + 0.02 * jax.random.normal(k, shape, f32)

    x = jax.random.normal(ks[0], (BATCH, SEQ, D), f32)
    w_in = jnp.concatenate([
        nrm(ks[1], (L, D, D_SB), std_d),
        nrm(ks[2], (L, D, D_SB), std_d),
        nrm(ks[3], (L, D, D_SB), std_d * BETA_INIT),
        nrm(ks[4], (L, D, D_CA), std_d),
        nrm(ks[5], (L, D, D_CA), std_d),
        nrm(ks[6], (L, D, D_CA), std_d * BETA_INIT),
    ], axis=-1)
    return {
        "x": x,
        "ffn1_w_gate": nrm(ks[7], (L, D, F), std_d),
        "ffn1_w_up": nrm(ks[8], (L, D, F), std_d),
        "ffn1_w_down": nrm(ks[9], (L, F, D), std_f * BETA_INIT),
        "ln1_g": gain(ks[10], (L, D)),
        "ln1_b": 0.02 * jax.random.normal(ks[11], (L, D), f32),
        "w_in": w_in,
        "rel_bias": 0.1 * jax.random.normal(ks[12], (L, H_CA, 2 * MAX_REL + 1), f32),
        "sb_out_g": gain(ks[13], (L, D_SB)),
        "ca_out_g": gain(ks[14], (L, D_CA)),
        "w_out": nrm(ks[15], (L, MIX_WIDTH, D), MIX_WIDTH ** -0.5 * BETA_INIT),
        "ln2_g": gain(ks[16], (L, D)),
        "ln2_b": 0.02 * jax.random.normal(ks[17], (L, D), f32),
        "ffn2_w_gate": nrm(ks[18], (L, D, F), std_d),
        "ffn2_w_up": nrm(ks[19], (L, D, F), std_d),
        "ffn2_w_down": nrm(ks[20], (L, F, D), std_f * BETA_INIT),
        "ln3_g": gain(ks[21], (L, D)),
        "ln3_b": 0.02 * jax.random.normal(ks[22], (L, D), f32),
    }

def reference(x, ffn1_w_gate, ffn1_w_up, ffn1_w_down, ln1_g, ln1_b, w_in, rel_bias,
              sb_out_g, ca_out_g, w_out, ln2_g, ln2_b, ffn2_w_gate, ffn2_w_up,
              ffn2_w_down, ln3_g, ln3_b):
    b, seq, _ = x.shape
    cuts = [D_SB, 2 * D_SB, 3 * D_SB, 3 * D_SB + D_CA, 3 * D_SB + 2 * D_CA]
    for l in range(DEPTH):
        x = layer_norm(ALPHA * x + FFN_RESIDUAL * swiglu(x, ffn1_w_gate[l], ffn1_w_up[l], ffn1_w_down[l]),
                       ln1_g[l], ln1_b[l])
        h = x @ w_in[l]
        qa, ka, va, qb, kb, vb = jnp.split(h, cuts, axis=-1)
        to_bhsd = lambda t, nh: t.reshape(b, seq, nh, HEAD_DIM).transpose(0, 2, 1, 3)
        oa = stick_breaking_attention(to_bhsd(qa, H_SB), to_bhsd(ka, H_SB), to_bhsd(va, H_SB))
        oa = oa.transpose(0, 2, 1, 3)
        to_bshd = lambda t, nh: t.reshape(b, seq, nh, HEAD_DIM)
        ob = chunked_rel_attention(to_bshd(qb, H_CA), to_bshd(kb, H_CA), to_bshd(vb, H_CA), rel_bias[l])
        mixed = jnp.concatenate([head_rmsnorm(oa, sb_out_g[l]), head_rmsnorm(ob, ca_out_g[l])], axis=-1)
        x = layer_norm(ALPHA * x + mixed @ w_out[l], ln2_g[l], ln2_b[l])
        x = layer_norm(ALPHA * x + FFN_RESIDUAL * swiglu(x, ffn2_w_gate[l], ffn2_w_up[l], ffn2_w_down[l]),
                       ln3_g[l], ln3_b[l])
    return x


_drawn_inputs = setup_inputs


def setup_inputs(seed=0):
    import zlib

    import numpy as np

    out = dict(_drawn_inputs(seed))
    spreads = {}
    factors = {}
    for name, (base, spread) in spreads.items():
        noise = np.random.default_rng([zlib.crc32(name.encode()), seed]).standard_normal(out[name].shape)
        drawn = base * np.exp(spread * noise) if base else spread * noise
        out[name] = __import__('jax').numpy.asarray(drawn.astype(out[name].dtype))
    for name, factor in factors.items():
        out[name] = (out[name] * factor).astype(out[name].dtype)
    return out
```

```python
from contextlib import ExitStack

import numpy as np

import concourse.bass as bass
from concourse import mybir

ALU = mybir.AluOpType
ACT = mybir.ActivationFunctionType
F32 = mybir.dt.float32
F32R = mybir.dt.float32r
I32 = mybir.dt.int32
AX_X = mybir.AxisListType.X

P = 128
D = 1024
T = 256
DEPTH = 2
F = 2816
HD = 64
HEADS = 8
MAX_REL = 128
BAND = 2 * MAX_REL + P
KC = D // P
FP = F // (2 * P)
UW = 2048
LN_EPS = 1e-5
RMS_EPS = 1e-6
ALPHA = float((2 * DEPTH) ** 0.25)
QSCALE = 1.0 / 8.0
NEG = -3.0e38
RSQRT_SEED = float(0x5F3759DF)

FFN_UNITS = 3 * FP
WIN_UNITS = 12
WOUT_UNITS = 4
UNITS = 2 * FFN_UNITS + WIN_UNITS + WOUT_UNITS
ATT0 = FFN_UNITS
FFN_BASE = (0, FFN_UNITS + WIN_UNITS + WOUT_UNITS)


def unit_slots():
    order = [n % 3 for n in range(FFN_UNITS)]
    order += [a % 3 for a in range(WIN_UNITS)] + [(2 + a) % 3 for a in range(WOUT_UNITS)]
    order += [n % 3 for n in range(FFN_UNITS)]
    seen, before = [0, 0, 0], []
    for s in order:
        before.append(seen[s])
        seen[s] += 1
    return order, before, seen


SLOT, FILLED, PER_LAYER = unit_slots()

SB_BANKS = [(1, (0, 1, 2, 3)), (0, (0, 1)), (0, (2, 3)), (1, (4, 5, 6, 7)), (0, (4, 5)), (0, (6, 7))]
SB_LATER = {1: 0, 2: 0, 4: 3, 5: 3}
CA_BANKS = [(0, (0, 1, 2, 3)), (0, (4, 5, 6, 7)), (1, (0, 1)), (1, (2, 3)), (1, (4, 5)), (1, (6, 7))]


def trunk(nc, x_in, stream, ln_gb, mix_g, rel_band, out):
    ctx = ExitStack()
    with ctx:
        def sb(name, shape, dt=F32):
            return ctx.enter_context(nc.sbuf_tensor(name, shape, dt))

        def sem(name):
            return ctx.enter_context(nc.semaphore(name))

        raw = sb("raw", [P, 3, UW])
        w_hi = sb("w_hi", [P, 3, UW], F32R)
        w_lo = sb("w_lo", [P, 3, UW], F32R)
        xT_hi = sb("xT_hi", [P, KC, T], F32R)
        xT_lo = sb("xT_lo", [P, KC, T], F32R)
        xn = sb("xn", [P, 2, D])
        xa = sb("xa", [P, 2, D])
        sg = sb("sg", [P, 512])
        hf = sb("hf", [P, 512])
        h_hi = sb("h_hi", [P, 2, T], F32R)
        h_lo = sb("h_lo", [P, 2, T], F32R)
        hl_hi = sb("hl_hi", [P, 2, T], F32R)
        hl_lo = sb("hl_lo", [P, 2, T], F32R)
        lnp = sb("lnp", [P, 2, D])
        mixg = sb("mixg", [P, D])
        band = sb("band", [P, HEADS, T])
        qT = sb("qT", [P, 8, T])
        kpad = sb("kpad", [P, 16, T])
        v = sb("v", [P, 2, D])
        ez = sb("ez", [P, 2, 512])
        sp_t = sb("sp_t", [P, 6, 512])
        pr_t = sb("pr_t", [P, 6, 512])
        pT = sb("pT", [P, 2, 512])
        ident = sb("ident", [P, P])
        neg_tri = sb("neg_tri", [P, P])
        neg_one = sb("neg_one", [P, P])
        flip = sb("flip", [P, P])
        stats = sb("stats", [P, 2, 6])
        mv = sb("mv", [P, 2])
        lt = sb("lt", [P, 8])
        mx = sb("mx", [P, 16])
        nmx = sb("nmx", [P, 16])
        se = sb("se", [P, 16])
        rinv = sb("rinv", [P, 16])
        hn = sb("hn", [P, 6, 16])

        bank = [ctx.enter_context(nc.psum_tensor(f"bank{i}", [P, 512], F32)) for i in range(8)]
        Y = [[bank[4], bank[5]], [bank[6], bank[7]]]
        Z = [bank[2], bank[3], bank[6]]

        raw_ready = [sem(f"raw_ready{s}") for s in range(3)]
        hi_ready = sem("hi_ready")
        lo_ready = sem("lo_ready")
        unit_used = sem("unit_used")
        x_loaded = sem("x_loaded")
        consts = sem("consts")
        kzero = sem("kzero")
        pool_steps = sem("pool_steps")
        dve_steps = sem("dve_steps")
        xn_done = sem("xn_done")
        xa_done = sem("xa_done")
        xt_done = sem("xt_done")
        xhi_done = sem("xhi_done")
        xlo_done = sem("xlo_done")
        y0_done = sem("y0_done")
        silu_done = sem("silu_done")
        hf_done = sem("hf_done")
        hhi_done = sem("hhi_done")
        hlo_done = sem("hlo_done")
        lnp_ready = sem("lnp_ready")
        att_par = sem("att_par")
        band_ready = sem("band_ready")
        band_mm = sem("band_mm")
        band_turned = sem("band_turned")
        ln_step = sem("ln_step")
        cent = sem("cent")
        unit_evac = sem("unit_evac")
        z_done = sem("z_done")
        az_done = sem("az_done")
        ez_done = sem("ez_done")
        lz_done = sem("lz_done")
        sp_done = sem("sp_done")
        spm_done = sem("spm_done")
        c_done = sem("c_done")
        w_done = sem("w_done")
        wm_done = sem("wm_done")
        oa_done = sem("oa_done")
        t_done = sem("t_done")
        sa_done = sem("sa_done")
        mx_done = sem("mx_done")
        nm_done = sem("nm_done")
        p_done = sem("p_done")
        x_done = sem("x_done")
        pt_done = sem("pt_done")
        vb_done = sem("vb_done")
        hn_o = sem("hn_o")
        hn_sq = sem("hn_sq")
        hn_step = sem("hn_step")
        mixed_done = sem("mixed_done")
        mt_done = sem("mt_done")
        mhi_done = sem("mhi_done")
        mlo_done = sem("mlo_done")
        stored = sem("stored")

        def used(l, rel):
            return l * UNITS + (rel + 4)

        def split(l, rel):
            return l * UNITS + (rel + 4)

        def it(l, f, j):
            return l * (2 * FP) + (f * FP) + j

        def phase(l, p):
            return l * 3 + p

        block = ctx.enter_context(nc.Block())

        @block.sync
        def _(sp):
            def load(slot, n, back=3):
                sp.wait_ge(lo_ready, n + (4 - back))
                sp.dma_start(raw[:, slot, :], stream[n]).then_inc(raw_ready[slot], 16)

            sp.dma_start(xn[:, :, :], x_in.rearrange("(b p) d -> p b d", p=P)).then_inc(x_loaded, 16)
            sp.sem_inc(lo_ready, 3)
            with sp.Fori(0, DEPTH) as l:
                with sp.Fori(0, (FFN_UNITS + WIN_UNITS) // 3) as i:
                    for s in range(3):
                        load(s, l * UNITS + i * 3 + s)
                for a in range(WOUT_UNITS):
                    rel = ATT0 + WIN_UNITS + a
                    load(SLOT[rel], l * UNITS + rel, back=1 if a == 0 else 3)
                with sp.Fori(0, FFN_UNITS // 3) as i:
                    for s in range(3):
                        load(s, l * UNITS + FFN_BASE[1] + i * 3 + s)
            sp.wait_ge(lo_ready, DEPTH * UNITS + 1)
            sp.dma_start(raw[:, 0, :], stream[DEPTH * UNITS - 1]).then_inc(raw_ready[0], 16)
            sp.wait_ge(xn_done, 2 * 3 * DEPTH)
            sp.dma_start(out.rearrange("(b p) d -> p b d", p=P), xn[:, :, :]).then_inc(stored, 16)
            sp.wait_ge(stored, 16)

        @block.gpsimd
        def _(pool):
            nc.gpsimd.memset(ident[:, :], 0.0).then_inc(consts, 1)
            nc.gpsimd.memset(neg_tri[:, :], -1.0).then_inc(consts, 1)
            nc.gpsimd.memset(neg_one[:, :], -1.0).then_inc(consts, 1)
            nc.gpsimd.memset(flip[:, :], 0.0).then_inc(consts, 1)
            pool.wait_ge(consts, 4)
            nc.gpsimd.affine_select(out=ident[:, :], in_=ident[:, :], compare_op=ALU.not_equal, fill=1.0,
                                    base=0, pattern=[[-1, P]], channel_multiplier=1).then_inc(consts, 1)
            nc.gpsimd.affine_select(out=neg_tri[:, :], in_=neg_tri[:, :], compare_op=ALU.is_ge, fill=0.0,
                                    base=0, pattern=[[-1, P]], channel_multiplier=1).then_inc(consts, 1)
            nc.gpsimd.affine_select(out=flip[:, :], in_=flip[:, :], compare_op=ALU.not_equal, fill=1.0,
                                    base=1 - P, pattern=[[1, P]], channel_multiplier=1).then_inc(consts, 1)
            nc.gpsimd.memset(kpad[:, :, :], 0.0).then_inc(kzero, 1)

            def load_lnp(n):
                pool.dma_start(lnp[:, :, :], ln_gb[n].partition_broadcast(P)).then_inc(lnp_ready, 16)

            def wait_alone(semaphore, value):
                pool.wait_ge(semaphore, value)
                pool.sem_inc(pool_steps, 1)

            def scale_x(count):
                for tb in range(2):
                    nc.gpsimd.tensor_scalar(xa[:, tb, :], xn[:, tb, :], ALPHA, None,
                                            ALU.mult).then_inc(xa_done, 1)

            def after_ln(l, p):
                for tb in range(2):
                    wait_alone(xn_done, phase(l, p) * 2 + (tb + 1))
                    nc.gpsimd.tensor_scalar(xa[:, tb, :], xn[:, tb, :], ALPHA, None,
                                            ALU.mult).then_inc(xa_done, 1)

            def causal(tiles, b, done):
                kb, heads = SB_BANKS[b]
                if kb == 1:
                    view = tiles[:, b, :].rearrange("p (h t) -> p h t", h=4)
                else:
                    view = tiles[:, b, :].rearrange("p (h t) -> p h t", h=2)[:, :, 0:P]
                nc.gpsimd.affine_select(out=view, in_=view, compare_op=ALU.is_gt, fill=0.0, base=0,
                                        pattern=[[0, len(heads)], [1, P]],
                                        channel_multiplier=-1).then_inc(done, 1)

            load_lnp(0)
            pool.wait_ge(x_loaded, 16)
            scale_x(0)
            with pool.Fori(0, DEPTH) as l:
                pool.dma_start(mixg[:, :], mix_g[l].partition_broadcast(P)).then_inc(att_par, 16)
                src = bass.AP(rel_band.tensor, l * (HEADS * BAND), [[1, P], [BAND, HEADS], [1, T]])
                pool.dma_start(sp_t[:, 0:4, :].rearrange("p a t -> p (a t)").rearrange(
                    "p (h s) -> p h s", h=HEADS), src).then_inc(att_par, 16)
                wait_alone(band_turned, (l + 1) * 4)
                nc.gpsimd.memset(band[0:64, :, 192:256], NEG).then_inc(band_ready, 1)
                after_ln(l, 0)
                load_lnp(l * 3 + 1)
                for b in range(7):
                    if b < 6:
                        wait_alone(sp_done, l * 6 + (b + 1))
                        causal(sp_t, b, spm_done)
                    if b > 0:
                        wait_alone(w_done, l * 6 + b)
                        causal(pr_t, b - 1, wm_done)
                after_ln(l, 1)
                load_lnp(l * 3 + 2)
                after_ln(l, 2)
                load_lnp((l + 1) * 3)

        @block.scalar
        def _(act):
            act.sem_inc(unit_used, 3)

            def split_hi(l, rel, slot, filled):
                act.wait_ge(raw_ready[slot], l * (16 * PER_LAYER[slot]) + 16 * (filled + 1))
                act.wait_ge(unit_used, used(l, rel - 3))
                nc.scalar.activation(w_hi[:, slot, :], raw[:, slot, :], ACT.Copy).then_inc(hi_ready, 1)

            def split_hi_at(l, rel):
                if rel == ATT0 + WIN_UNITS:
                    act.wait_ge(unit_used, used(l, rel - 1))
                split_hi(l, rel, SLOT[rel], FILLED[rel])

            def x_hi(count):
                for g in range(4):
                    tb, half = divmod(g, 2)
                    act.wait_ge(xt_done, count * 4 + (g + 1))
                    nc.scalar.activation(xT_hi[:, 4 * half:4 * half + 4, tb * P:(tb + 1) * P],
                                         bank[g][:, :].rearrange("p (c t) -> p c t", c=4),
                                         ACT.Copy).then_inc(xhi_done, 1)

            def ffn(l, f):
                base = FFN_BASE[f]
                first = FILLED[base:base + 3]

                def silu(j, rel):
                    act.wait_ge(unit_used, used(l, base + rel))
                    nc.scalar.activation(sg[:, :], bank[0][:, :], ACT.Silu).then_inc(silu_done, 1)

                split_hi(l, base + 1, 1, first[1])
                split_hi(l, base + 2, 2, first[2])
                silu(0, 0)
                split_hi(l, base + 3, 0, first[0] + 1)
                with act.Fori(0, FP - 1) as j:
                    act.wait_ge(hf_done, it(l, f, j) + 1)
                    act.wait_ge(unit_used, used(l, base + 3 * j + 1))
                    nc.scalar.activation(h_hi[:, :, :], hf[:, :].rearrange("p (c t) -> p c t", c=2),
                                         ACT.Copy).then_inc(hhi_done, 1)
                    split_hi(l, base + 3 * j + 4, 1, first[1] + 1 + j)
                    split_hi(l, base + 3 * j + 5, 2, first[2] + 1 + j)
                    silu(j + 1, 3 * j + 2)
                    split_hi(l, base + 3 * j + 6, 0, first[0] + 2 + j)
                act.wait_ge(hf_done, it(l, f, FP))
                nc.scalar.activation(hl_hi[:, :, :], hf[:, :].rearrange("p (c t) -> p c t", c=2),
                                     ACT.Copy).then_inc(hhi_done, 1)

            def evacuate(l, a):
                part, kind = divmod(a, 6)
                two = bank[a % 2][:, :].rearrange("p (c t) -> p c t", c=2)
                act.wait_ge(unit_used, used(l, ATT0 + a))
                if kind < 2:
                    nc.scalar.activation(qT[:, 4 * part + 2 * kind:4 * part + 2 * kind + 2, :], two,
                                         ACT.Copy, scale=QSCALE).then_inc(unit_evac, 1)
                elif kind < 4:
                    h0 = 8 * part + 4 * (kind - 2)
                    nc.scalar.activation(kpad[0:64, h0:h0 + 4:2, :], two[0:64], ACT.Copy)
                    nc.scalar.activation(kpad[64:128, h0 + 1:h0 + 4:2, :], two[64:128],
                                         ACT.Copy).then_inc(unit_evac, 1)
                else:
                    c0 = 512 * part + 256 * (kind - 4)
                    nc.scalar.activation(v[:, :, c0:c0 + 256], two, ACT.Copy).then_inc(unit_evac, 1)

            def log_keep(l, b):
                e = ez[:, b % 2, :]
                act.wait_ge(z_done, l * 6 + (b + 1))
                if b >= 2:
                    act.wait_ge(sp_done, l * 6 + (b - 1))
                nc.scalar.activation(e, Z[b % 3][:, :], ACT.Abs).then_inc(az_done, 1)
                act.wait_ge(az_done, l * 6 + (b + 1))
                nc.scalar.activation(e, e, ACT.Exp, scale=-1.0).then_inc(ez_done, 1)
                act.wait_ge(ez_done, l * 6 + (b + 1))
                nc.scalar.activation(e, e, ACT.Ln, bias=1.0).then_inc(lz_done, 1)

            def weights(l, b):
                act.wait_ge(c_done, l * 6 + (b + 1))
                nc.scalar.activation(pr_t[:, b, :], Z[b % 3][:, :], ACT.Exp).then_inc(w_done, 1)

            def softmax_exp(l, b):
                qb, heads = CA_BANKS[b]
                n = 512 // len(heads)
                act.wait_ge(nm_done, l * 6 + (b + 1))
                for i, h in enumerate(heads):
                    c = 8 * qb + h
                    last = nc.scalar.activation(pr_t[:, b, i * n:(i + 1) * n], sp_t[:, b, i * n:(i + 1) * n],
                                                ACT.Exp, bias=nmx[:, c:c + 1], accum_out=se[:, c:c + 1])
                last.then_inc(p_done, 1)

            def square(l, part):
                for qb in range(2):
                    act.wait_ge(hn_o, l * 4 + (2 * part + qb + 1))
                    nc.scalar.activation(ez[:, qb, :], xn[:, qb, 512 * part:512 * part + 512],
                                         ACT.Square).then_inc(hn_sq, 1)

            def mixed_hi(l, part):
                for qb in range(2):
                    g = 2 * part + qb
                    act.wait_ge(mt_done, l * 4 + (g + 1))
                    nc.scalar.activation(xT_hi[:, 4 * part:4 * part + 4, qb * P:(qb + 1) * P],
                                         bank[g][:, :].rearrange("p (c t) -> p c t", c=4),
                                         ACT.Copy).then_inc(mhi_done, 1)

            def attention(l):
                act.wait_ge(kzero, 1)
                split_hi_at(l, ATT0 + 1)
                split_hi_at(l, ATT0 + 2)
                for a in range(3):
                    evacuate(l, a)
                    split_hi_at(l, ATT0 + a + 3)
                for b in range(6):
                    evacuate(l, 3 + b)
                    split_hi_at(l, ATT0 + 6 + b)
                    log_keep(l, b)
                    if b > 0:
                        weights(l, b - 1)
                evacuate(l, 9)
                weights(l, 5)
                evacuate(l, 10)
                evacuate(l, 11)
                softmax_exp(l, 0)
                softmax_exp(l, 1)
                square(l, 0)
                split_hi_at(l, ATT0 + 12)
                softmax_exp(l, 2)
                softmax_exp(l, 3)
                split_hi_at(l, ATT0 + 13)
                softmax_exp(l, 4)
                softmax_exp(l, 5)
                split_hi_at(l, ATT0 + 14)
                mixed_hi(l, 0)
                square(l, 1)
                mixed_hi(l, 1)
                split_hi_at(l, ATT0 + 15)
                split_hi_at(l, ATT0 + 16)

            split_hi(0, 0, 0, 0)
            x_hi(0)
            with act.Fori(0, DEPTH) as l:
                ffn(l, 0)
                for i in range(4):
                    act.wait_ge(band_mm, l * 4 + (i + 1))
                    nc.scalar.activation(band[:, 2 * i:2 * i + 2, :],
                                         bank[i][:, :].rearrange("p (h s) -> p h s", h=2),
                                         ACT.Copy).then_inc(band_turned, 1)
                x_hi(phase(l, 1))
                attention(l)
                x_hi(phase(l, 2))
                ffn(l, 1)
                x_hi(phase(l, 3))

        @block.vector
        def _(dve):
            def split_lo(l, rel, slot):
                dve.wait_ge(hi_ready, l * UNITS + (rel + 1))
                nc.vector.tensor_tensor(w_lo[:, slot, :], raw[:, slot, :], w_hi[:, slot, :].bitcast(F32),
                                        ALU.subtract).then_inc(lo_ready, 1)

            def x_lo(count):
                for g in range(4):
                    tb, half = divmod(g, 2)
                    dve.wait_ge(xhi_done, count * 4 + (g + 1))
                    part = slice(4 * half, 4 * half + 4), slice(tb * P, (tb + 1) * P)
                    nc.vector.tensor_tensor(xT_lo[:, part[0], part[1]],
                                            bank[g][:, :].rearrange("p (c t) -> p c t", c=4),
                                            xT_hi[:, part[0], part[1]].bitcast(F32),
                                            ALU.subtract).then_inc(xlo_done, 1)

            LN_STEPS = 15

            def layer_norm(l, p):
                scale = 1.0 if p == 1 else 0.5
                end = (ATT0 - 1, FFN_BASE[1] - 1, UNITS - 1)[p]
                dve.wait_ge(lnp_ready, phase(l, p) * 16 + 16)
                for tb in range(2):
                    n = phase(l, p) * 2 + tb
                    k = [0]

                    def done(ins):
                        k[0] += 1
                        ins.then_inc(ln_step, 1)

                    def after(count):
                        dve.wait_ge(ln_step, n * LN_STEPS + count)

                    if tb == 0:
                        dve.wait_ge(y0_done, phase(l, p) + 1)
                    else:
                        dve.wait_ge(unit_used, used(l, end))
                    dve.wait_ge(xa_done, n + 1)
                    for half in range(2):
                        cols = slice(512 * half, 512 * half + 512)
                        done(nc.vector.scalar_tensor_tensor(out=xn[:, tb, cols], in0=Y[tb][half][:, :],
                                                            scalar=scale, in1=xa[:, tb, cols],
                                                            op0=ALU.mult, op1=ALU.add))
                    for half in range(2):
                        after(half + 1)
                        done(nc.vector.bn_stats(stats[:, half, :], xn[:, tb, 512 * half:512 * half + 512]))
                    after(4)
                    dve.sem_inc(dve_steps, 1)
                    done(nc.vector.bn_aggr(mv[:, :], stats[:, :, :].rearrange("p a b -> p (a b)")))
                    after(5)
                    done(nc.vector.tensor_scalar(lt[:, 0:1], mv[:, 1:2], LN_EPS, None, ALU.add))
                    done(nc.vector.tensor_scalar(lt[:, 1:2], mv[:, 1:2], LN_EPS, -0.5, ALU.add, ALU.mult))
                    after(6)
                    done(nc.vector.tensor_scalar(lt[:, 2:3].bitcast(I32), lt[:, 0:1].bitcast(I32), 1, None,
                                                 ALU.logical_shift_right))
                    after(8)
                    done(nc.vector.tensor_scalar(lt[:, 3:4].bitcast(I32), lt[:, 2:3].bitcast(I32), -1.0,
                                                 RSQRT_SEED, ALU.mult, ALU.add))
                    for step in range(3):
                        y, yn = lt[:, 3 + step:4 + step], lt[:, 4 + step:5 + step]
                        after(k[0])
                        t = lt[:, 2:3]
                        ins = nc.vector.tensor_scalar(t, y, y, lt[:, 1:2], ALU.mult, ALU.mult)
                        done(ins)
                        after(k[0])
                        ins = nc.vector.tensor_scalar(yn, t, 1.5, y, ALU.add, ALU.mult)
                        done(ins)
                    assert k[0] == LN_STEPS
                    after(k[0])
                    nc.vector.scalar_tensor_tensor(out=xn[:, tb, :], in0=xn[:, tb, :], scalar=mv[:, 0:1],
                                                   in1=lnp[:, 0, :], op0=ALU.subtract,
                                                   op1=ALU.mult).then_inc(cent, 1)
                    dve.wait_ge(cent, n + 1)
                    nc.vector.scalar_tensor_tensor(out=xn[:, tb, :], in0=xn[:, tb, :], scalar=lt[:, 6:7],
                                                   in1=lnp[:, 1, :], op0=ALU.mult,
                                                   op1=ALU.add).then_inc(xn_done, 1)

            def ffn(l, f):
                base = FFN_BASE[f]

                def gated(step, rel, first=False):
                    if not first:
                        dve.wait_ge(hlo_done, step)
                    dve.wait_ge(silu_done, step + 1)
                    dve.wait_ge(unit_used, used(l, base + rel))
                    nc.vector.tensor_tensor(hf[:, :], sg[:, :], bank[1][:, :], ALU.mult).then_inc(hf_done, 1)

                def h_low(step, hi, lo):
                    dve.wait_ge(hhi_done, step + 1)
                    nc.vector.tensor_tensor(lo[:, :, :], hf[:, :].rearrange("p (c t) -> p c t", c=2),
                                            hi[:, :, :].bitcast(F32), ALU.subtract).then_inc(hlo_done, 1)

                split_lo(l, base + 1, 1)
                split_lo(l, base + 2, 2)
                gated(it(l, f, 0), 1, first=True)
                split_lo(l, base + 3, 0)
                with dve.Fori(0, FP - 1) as j:
                    h_low(it(l, f, j), h_hi, h_lo)
                    split_lo(l, base + 3 * j + 4, 1)
                    split_lo(l, base + 3 * j + 5, 2)
                    gated(it(l, f, j) + 1, 3 * j + 3)
                    split_lo(l, base + 3 * j + 6, 0)
                h_low(it(l, f, FP - 1), hl_hi, hl_lo)

            def split_lo_at(l, rel):
                split_lo(l, rel, SLOT[rel])

            def softplus(l, b):
                dve.wait_ge(lz_done, l * 6 + (b + 1))
                nc.vector.scalar_tensor_tensor(out=sp_t[:, b, :], in0=Z[b % 3][:, :], scalar=0.0,
                                               in1=ez[:, b % 2, :], op0=ALU.max,
                                               op1=ALU.add).then_inc(sp_done, 1)

            def scores(l, b):
                qb, heads = CA_BANKS[b]
                n, m = len(heads), 512 // len(heads)
                s = sp_t[:, b, :].rearrange("p (h s) -> p h s", h=n)
                c = slice(8 * qb + heads[0], 8 * qb + heads[0] + n)
                dve.wait_ge(t_done, l * 6 + (b + 1))
                nc.vector.tensor_tensor(s, Z[b % 2][:, :].rearrange("p (h s) -> p h s", h=n),
                                        band[:, heads[0]:heads[0] + n, T - m:T], ALU.add).then_inc(sa_done, 1)
                dve.wait_ge(sa_done, l * 6 + (b + 1))
                nc.vector.tensor_reduce(mx[:, c], s, AX_X, ALU.max).then_inc(mx_done, 1)
                dve.wait_ge(mx_done, l * 6 + (b + 1))
                nc.vector.tensor_scalar(nmx[:, c], mx[:, c], -1.0, None, ALU.mult).then_inc(nm_done, 1)

            def turned(l, b):
                dve.wait_ge(x_done, l * 6 + (b + 1))
                if b >= 2:
                    dve.wait_ge(vb_done, l * 6 + (b - 1))
                nc.vector.tensor_copy(pT[:, b % 2, :], bank[6 + b % 2][:, :]).then_inc(pt_done, 1)

            HN_STEPS = (17, 18)

            def head_norm(l, part):
                k = [0]

                def link(ins, wait=True):
                    k[0] += 1
                    ins.then_inc(hn_step, 1)
                    if wait:
                        dve.wait_ge(hn_step, l * sum(HN_STEPS) + (part * HN_STEPS[0] + k[0]))

                if part == 0:
                    dve.wait_ge(oa_done, l + 1)
                    dve.wait_ge(xa_done, phase(l, 1) * 2 + 2)
                    dve.wait_ge(att_par, (l + 1) * 32)
                else:
                    dve.wait_ge(p_done, (l + 1) * 6)
                    link(nc.vector.reciprocal(rinv[:, :], se[:, :]))
                    dve.wait_ge(vb_done, (l + 1) * 6)
                cols = slice(512 * part, 512 * part + 512)

                def heads(t):
                    return t.rearrange("p (h d) -> p h d", h=HEADS)

                for qb in range(2):
                    o = bank[4 + qb][:, :]
                    if part == 0:
                        nc.vector.tensor_copy(xn[:, qb, cols], o).then_inc(hn_o, 1)
                    else:
                        r = rinv[:, 8 * qb:8 * qb + 8].unsqueeze(2).to_broadcast([P, HEADS, HD])
                        nc.vector.tensor_tensor(heads(xn[:, qb, cols]), heads(o), r, ALU.mult).then_inc(hn_o, 1)
                for qb in range(2):
                    dve.wait_ge(hn_sq, l * 4 + (2 * part + qb + 1))
                    link(nc.vector.tensor_reduce(hn[:, 0, 8 * qb:8 * qb + 8], heads(ez[:, qb, :]), AX_X,
                                                 ALU.add), wait=qb == 1)
                link(nc.vector.tensor_scalar(hn[:, 1, :], hn[:, 0, :], 1.0 / HD, RMS_EPS, ALU.mult, ALU.add))
                link(nc.vector.tensor_scalar(hn[:, 2, :], hn[:, 1, :], -0.5, None, ALU.mult))
                link(nc.vector.tensor_scalar(hn[:, 3, :].bitcast(I32), hn[:, 1, :].bitcast(I32), 1, None,
                                             ALU.logical_shift_right))
                link(nc.vector.tensor_scalar(hn[:, 4, :].bitcast(I32), hn[:, 3, :].bitcast(I32), -1.0,
                                             RSQRT_SEED, ALU.mult, ALU.add))
                y = 4
                for step in range(3):
                    link(nc.vector.tensor_tensor(hn[:, 3, :], hn[:, y, :], hn[:, y, :], ALU.mult))
                    link(nc.vector.tensor_tensor(hn[:, 3, :], hn[:, 3, :], hn[:, 2, :], ALU.mult))
                    link(nc.vector.scalar_tensor_tensor(out=hn[:, 9 - y, :], in0=hn[:, 3, :], scalar=1.5,
                                                        in1=hn[:, y, :], op0=ALU.add, op1=ALU.mult))
                    y = 9 - y
                for qb in range(2):
                    r = hn[:, y, 8 * qb:8 * qb + 8].unsqueeze(2).to_broadcast([P, HEADS, HD])
                    link(nc.vector.tensor_tensor(heads(xn[:, qb, cols]), heads(xn[:, qb, cols]), r, ALU.mult))
                    nc.vector.tensor_tensor(xn[:, qb, cols], xn[:, qb, cols], mixg[:, cols],
                                            ALU.mult).then_inc(mixed_done, 1)
                assert k[0] == (HN_STEPS[part]), k

            def mixed_lo(l, part):
                for qb in range(2):
                    g = 2 * part + qb
                    dve.wait_ge(mhi_done, l * 4 + (g + 1))
                    where = slice(4 * part, 4 * part + 4), slice(qb * P, (qb + 1) * P)
                    nc.vector.tensor_tensor(xT_lo[:, where[0], where[1]],
                                            bank[g][:, :].rearrange("p (c t) -> p c t", c=4),
                                            xT_hi[:, where[0], where[1]].bitcast(F32),
                                            ALU.subtract).then_inc(mlo_done, 1)

            def attention(l):
                for rel in range(1, 6):
                    split_lo_at(l, ATT0 + rel)
                for b in range(6):
                    split_lo_at(l, ATT0 + 6 + b)
                    softplus(l, b)
                dve.wait_ge(band_ready, l + 1)
                scores(l, 0)
                scores(l, 1)
                head_norm(l, 0)
                split_lo_at(l, ATT0 + 12)
                turned(l, 0)
                turned(l, 1)
                scores(l, 2)
                scores(l, 3)
                split_lo_at(l, ATT0 + 13)
                turned(l, 2)
                turned(l, 3)
                scores(l, 4)
                scores(l, 5)
                split_lo_at(l, ATT0 + 14)
                turned(l, 4)
                turned(l, 5)
                mixed_lo(l, 0)
                head_norm(l, 1)
                mixed_lo(l, 1)
                split_lo_at(l, ATT0 + 15)
                split_lo_at(l, ATT0 + 16)

            split_lo(0, 0, 0)
            x_lo(0)
            with dve.Fori(0, DEPTH) as l:
                ffn(l, 0)
                layer_norm(l, 0)
                x_lo(phase(l, 1))
                attention(l)
                layer_norm(l, 1)
                x_lo(phase(l, 2))
                ffn(l, 1)
                layer_norm(l, 2)
                x_lo(phase(l, 3))

        @block.tensor
        def _(pe):
            def three(o, w, x, start, stop):
                nc.tensor.matmul(o, w[0], x[0], start=start, stop=False)
                nc.tensor.matmul(o, w[0], x[1], start=False, stop=False)
                return nc.tensor.matmul(o, w[1], x[0], start=False, stop=stop)

            def columns(l, rel, slot, out_bank, last_inc=True):
                pe.wait_ge(lo_ready, split(l, rel))
                for c in range(2):
                    for kc in range(KC):
                        w = slice(kc * 256 + c * P, kc * 256 + (c + 1) * P)
                        last = three(out_bank[:, c * T:(c + 1) * T], (w_hi[:, slot, w], w_lo[:, slot, w]),
                                     (xT_hi[:, kc, :], xT_lo[:, kc, :]), kc == 0, kc == KC - 1)
                last.then_inc(unit_used, 1)

            def rows(l, rel, slot, out_bank):
                pe.wait_ge(lo_ready, split(l, rel))
                for tb in range(2):
                    for kc in range(KC):
                        w = slice(kc * 256, (kc + 1) * 256)
                        t = slice(tb * P, (tb + 1) * P)
                        last = three(out_bank[:, tb * 256:(tb + 1) * 256], (xT_hi[:, kc, t], xT_lo[:, kc, t]),
                                     (w_hi[:, slot, w], w_lo[:, slot, w]), kc == 0, kc == KC - 1)
                last.then_inc(unit_used, 1)

            def down(slot, hi, lo, c0, tbs, start=False, stop=False):
                for tb in tbs:
                    for half in range(2):
                        for c in range(2):
                            w = slice(c * D + half * 512, c * D + half * 512 + 512)
                            t = slice(tb * P, (tb + 1) * P)
                            last = three(Y[tb][half][:, :], (hi[:, c0 + c, t], lo[:, c0 + c, t]),
                                         (w_hi[:, slot, w], w_lo[:, slot, w]),
                                         start and c == 0, stop and c == 1)
                return last

            def turn_x(count, band_turned_by=None):
                for g in range(4):
                    tb, half = divmod(g, 2)
                    if count is not None and half == 0:
                        pe.wait_ge(xn_done, count * 2 + (tb - 1))
                        if band_turned_by is not None:
                            pe.wait_ge(band_turned, band_turned_by)
                    for q in range(4):
                        c = (4 * half + q) * P
                        last = nc.tensor.transpose(bank[g][:, q * P:(q + 1) * P], xn[:, tb, c:c + P], ident[:, :])
                    last.then_inc(xt_done, 1)

            def turn_band(l):
                pe.wait_ge(att_par, (l + 1) * 32)
                pe.wait_ge(hf_done, it(l, 0, FP))
                for i in range(4):
                    nc.tensor.matmul(bank[i][:, :], flip[:, :], sp_t[:, i, :], start=True,
                                     stop=True).then_inc(band_mm, 1)

            def ffn(l, f, count):
                base = FFN_BASE[f]
                pe.wait_ge(xlo_done, count * 4 + 4)
                columns(l, base, 0, bank[0])
                columns(l, base + 1, 1, bank[1])

                def gate_up(j):
                    pe.wait_ge(silu_done, it(l, f, j) + 1)
                    columns(l, base + 3 * j + 2, 2, bank[0])
                    pe.wait_ge(hf_done, it(l, f, j) + 1)
                    columns(l, base + 3 * j + 3, 0, bank[1])

                def step(j, start):
                    gate_up(j)
                    pe.wait_ge(hlo_done, it(l, f, j) + 1)
                    pe.wait_ge(lo_ready, split(l, base + 3 * j + 4))
                    down(1, h_hi, h_lo, 0, (0, 1), start=start).then_inc(unit_used, 1)

                step(0, True)
                with pe.Fori(1, FP - 2) as j:
                    step(j, False)
                gate_up(FP - 2)
                pe.wait_ge(hlo_done, it(l, f, FP))
                pe.wait_ge(lo_ready, split(l, base + FFN_UNITS - 1))
                down(1, h_hi, h_lo, 0, (0,))
                down(2, hl_hi, hl_lo, 0, (0,), stop=True).then_inc(y0_done, 1)
                down(1, h_hi, h_lo, 0, (1,)).then_inc(unit_used, 1)
                down(2, hl_hi, hl_lo, 0, (1,), stop=True).then_inc(unit_used, 1)

            def plain(o, w, x, start=False, stop=False):
                return nc.tensor.matmul(o, w, x, start=start, stop=stop, skip_group_check=True)

            def sb_scores(l, b):
                kb, heads = SB_BANKS[b]
                if b == 0:
                    pe.wait_ge(unit_evac, l * WIN_UNITS + 4)
                if b >= 3:
                    pe.wait_ge(w_done, l * 6 + (b - 2))
                m = 512 // len(heads)
                for i, h in enumerate(heads):
                    last = plain(Z[b % 3][:, i * m:(i + 1) * m], kpad[:, h, kb * P:(kb + 1) * P],
                                 qT[:, h // 2, T - m:T], start=i == 0)
                last.then_inc(z_done, 1)

            def sb_sums(l, b):
                kb, heads = SB_BANKS[b]
                z = Z[b % 3]
                pe.wait_ge(spm_done, l * 6 + (b + 1))
                last = plain(z[:, :], neg_tri[:, :], sp_t[:, b, :], stop=kb == 1)
                if kb == 0:
                    for i, h in enumerate(heads):
                        j = SB_BANKS[SB_LATER[b]][1].index(h)
                        last = plain(z[:, i * T + P:(i + 1) * T], neg_one[:, :],
                                     sp_t[:, SB_LATER[b], j * P:(j + 1) * P], stop=i == len(heads) - 1)
                last.then_inc(c_done, 1)

            def sb_values(l, b):
                _, heads = SB_BANKS[b]
                pe.wait_ge(wm_done, l * 6 + (b + 1))
                pe.wait_ge(unit_evac, l * WIN_UNITS + 6)
                for i, h in enumerate(heads):
                    j = SB_BANKS[SB_LATER[b]][1].index(h)
                    o = slice(h * HD, (h + 1) * HD)
                    plain(bank[4][:, o], pr_t[:, b, i * T:i * T + P], v[:, 0, o], start=True, stop=True)
                    plain(bank[5][:, o], pr_t[:, b, i * T + P:(i + 1) * T], v[:, 0, o], start=True)
                    last = plain(bank[5][:, o], pr_t[:, SB_LATER[b], j * P:(j + 1) * P], v[:, 1, o], stop=True)
                if b == 5:
                    last.then_inc(oa_done, 1)

            def ca_scores(l, b):
                qb, heads = CA_BANKS[b]
                if b == 0:
                    pe.wait_ge(unit_evac, l * WIN_UNITS + 10)
                if b < 2:
                    pe.wait_ge(w_done, l * 6 + (b + 4))
                else:
                    pe.wait_ge(sa_done, l * 6 + (b - 1))
                m = 512 // len(heads)
                for i, h in enumerate(heads):
                    last = plain(Z[b % 2][:, i * m:(i + 1) * m], qT[:, 4 + h // 2, qb * P:(qb + 1) * P],
                                 kpad[:, 8 + h, 0:m], start=True, stop=True)
                last.then_inc(t_done, 1)

            def ca_turn(l, b):
                pe.wait_ge(p_done, l * 6 + (b + 1))
                if b == 0:
                    pe.wait_ge(w_done, (l + 1) * 6)
                if b >= 2:
                    pe.wait_ge(pt_done, l * 6 + (b - 1))
                for q in range(4):
                    last = nc.tensor.transpose(bank[6 + b % 2][:, q * P:(q + 1) * P],
                                               pr_t[:, b, q * P:(q + 1) * P], ident[:, :])
                last.then_inc(x_done, 1)

            def ca_values(l, b):
                qb, heads = CA_BANKS[b]
                n = qb + 1
                pe.wait_ge(pt_done, l * 6 + (b + 1))
                if b == 0:
                    pe.wait_ge(hn_o, l * 4 + 2)
                    pe.wait_ge(unit_evac, (l + 1) * WIN_UNITS)
                for i, h in enumerate(heads):
                    o = slice(h * HD, (h + 1) * HD)
                    for kb in range(n):
                        c = (i * n + kb) * P
                        last = plain(bank[4 + qb][:, o], pT[:, b % 2, c:c + P],
                                     v[:, kb, 512 + h * HD:512 + (h + 1) * HD], start=kb == 0, stop=kb == n - 1)
                last.then_inc(vb_done, 1)

            def turn_mixed(l, part):
                for qb in range(2):
                    g = 2 * part + qb
                    pe.wait_ge(mixed_done, l * 4 + (g + 1))
                    for q in range(4):
                        c = (4 * part + q) * P
                        last = nc.tensor.transpose(bank[g][:, q * P:(q + 1) * P], xn[:, qb, c:c + P], ident[:, :])
                    last.then_inc(mt_done, 1)

            def w_in(l, a):
                if a >= 2:
                    pe.wait_ge(unit_evac, l * WIN_UNITS + (a - 1))
                f = rows if a % 6 >= 4 else columns
                f(l, ATT0 + a, SLOT[ATT0 + a], bank[a % 2])

            def attention(l):
                pe.wait_ge(xlo_done, phase(l, 1) * 4 + 4)
                for a in range(4):
                    w_in(l, a)
                sb_scores(l, 0)
                w_in(l, 4)
                sb_scores(l, 1)
                for b in range(6):
                    w_in(l, 5 + b)
                    sb_sums(l, b)
                    if b in (2, 3):
                        sb_values(l, b - 1)
                    if b == 5:
                        sb_values(l, 4)
                    if b < 4:
                        sb_scores(l, b + 2)
                w_in(l, 11)
                sb_values(l, 5)
                ca_scores(l, 0)
                ca_scores(l, 1)
                for b in (0, 2, 4):
                    ca_turn(l, b)
                    ca_turn(l, b + 1)
                    if b < 4:
                        ca_scores(l, b + 2)
                        ca_scores(l, b + 3)
                    ca_values(l, b)
                    ca_values(l, b + 1)
                turn_mixed(l, 0)
                turn_mixed(l, 1)
                pe.wait_ge(mlo_done, (l + 1) * 4)
                rels = [ATT0 + WIN_UNITS + i for i in range(WOUT_UNITS)]
                for i in range(2):
                    pe.wait_ge(lo_ready, split(l, rels[i]))
                    down(SLOT[rels[i]], xT_hi, xT_lo, 2 * i, (0, 1), start=i == 0).then_inc(unit_used, 1)
                pe.wait_ge(lo_ready, split(l, rels[3]))
                for tb in range(2):
                    for i in (2, 3):
                        last = down(SLOT[rels[i]], xT_hi, xT_lo, 2 * i, (tb,), stop=i == 3)
                        if tb == 0 and i == 3:
                            last.then_inc(y0_done, 1)
                        if tb == 1:
                            last.then_inc(unit_used, 1)

            pe.wait_ge(consts, 7)
            pe.wait_ge(x_loaded, 16)
            turn_x(None)
            with pe.Fori(0, DEPTH) as l:
                ffn(l, 0, phase(l, 0))
                turn_band(l)
                turn_x(phase(l, 1), (l + 1) * 4)
                attention(l)
                turn_x(phase(l, 2))
                ffn(l, 1, phase(l, 2))
                turn_x(phase(l, 3))


_ARGS = ["x", "ffn1_w_gate", "ffn1_w_up", "ffn1_w_down", "ln1_g", "ln1_b", "w_in", "rel_bias", "sb_out_g",
         "ca_out_g", "w_out", "ln2_g", "ln2_b", "ffn2_w_gate", "ffn2_w_up", "ffn2_w_down", "ln3_g", "ln3_b"]


def column_units(w):
    k, n = w.shape
    return w.reshape(k // P, P, n // 256, 256).transpose(2, 1, 0, 3).reshape(n // 256, P, UW)


def row_units(w):
    return w.reshape(w.shape[0] // 256, 2, P, D).transpose(0, 2, 1, 3).reshape(-1, P, UW)


def weight_stream(ins):
    units = []
    for l in range(DEPTH):
        for f in ("ffn1", "ffn2"):
            g, u = (column_units(ins[f"{f}_w_{k}"][l]) for k in ("gate", "up"))
            d = row_units(ins[f"{f}_w_down"][l])
            units += [g[0], u[0]]
            for j in range(FP - 1):
                units += [g[j + 1], u[j + 1], d[j]]
            units.append(d[FP - 1])
            if f == "ffn1":
                units += list(column_units(ins["w_in"][l])) + list(row_units(ins["w_out"][l]))
    return np.stack(units)


def kernel(**inputs):
    import concourse.bacc as bacc
    from concourse.bass_utils import run_bass_kernel_spmd

    ins = {k: np.asarray(inputs[k]) for k in _ARGS}
    ln = np.stack([np.stack([ins[f"ln{i}_{k}"] for k in "gb"], 1) for i in (1, 2, 3)], 1)
    ln = ln.reshape(DEPTH * 3, 2, D)
    ln = np.concatenate([ln, ln[:1]])
    mix = np.concatenate([ins["sb_out_g"], ins["ca_out_g"]], 1)
    flipped = ins["rel_bias"][:, :, ::-1]
    rel = np.concatenate([np.repeat(flipped[:, :, :1], P - 1, axis=2), flipped], 2)
    arrays = {
        "x": ins["x"].reshape(T, D),
        "stream": weight_stream(ins),
        "ln_gb": ln,
        "mix_g": mix,
        "rel_band": rel,
    }
    arrays = {k: np.ascontiguousarray(a) for k, a in arrays.items()}
    nc = bacc.Bacc("TRN2", target_bir_lowering=False, num_devices=1)
    args = [nc.dram_tensor(k, a.shape, F32, kind="ExternalInput").ap() for k, a in arrays.items()]
    out = nc.dram_tensor("out", (T, D), F32, kind="ExternalOutput").ap()
    trunk(nc, *args, out)
    r = run_bass_kernel_spmd(nc, [arrays], core_ids=[0])
    return r.results[0]["out"].reshape(1, T, D)
```

```python
from contextlib import ExitStack

import numpy as np

import concourse.bass as bass
from concourse import mybir

ALU = mybir.AluOpType
ACT = mybir.ActivationFunctionType
F32 = mybir.dt.float32
F32R = mybir.dt.float32r
I32 = mybir.dt.int32
AX_X = mybir.AxisListType.X

P = 128
D = 1024
T = 256
DEPTH = 2
F = 2816
HD = 64
HEADS = 8
MAX_REL = 128
BAND = 2 * MAX_REL + P
KC = D // P
FP = F // (2 * P)
UW = 2048
LN_EPS = 1e-5
RMS_EPS = 1e-6
ALPHA = float((2 * DEPTH) ** 0.25)
QSCALE = 1.0 / 8.0
NEG = -3.0e38
RSQRT_SEED = float(0x5F3759DF)

FFN_UNITS = 3 * FP
WIN_UNITS = 12
WOUT_UNITS = 4
UNITS = 2 * FFN_UNITS + WIN_UNITS + WOUT_UNITS
ATT0 = FFN_UNITS
FFN_BASE = (0, FFN_UNITS + WIN_UNITS + WOUT_UNITS)


def unit_slots():
    order = [n % 3 for n in range(FFN_UNITS)]
    order += [a % 3 for a in range(WIN_UNITS)] + [1, 0, 2, 1]
    order += [n % 3 for n in range(FFN_UNITS)]
    seen, before = [0, 0, 0], []
    for s in order:
        before.append(seen[s])
        seen[s] += 1
    return order, before, seen


LN_VARIANCE, LN_STEPS = 5, 10

SLOT, FILLED, PER_LAYER = unit_slots()

W_IN = [(kind, part, half) for kind, part in (("q", 0), ("k", 0), ("q", 1), ("k", 1), ("v", 0), ("v", 1))
        for half in range(2)]
SB_BANKS = [(1, (0, 1, 2, 3)), (0, (0, 1)), (0, (2, 3)), (1, (4, 5, 6, 7)), (0, (4, 5)), (0, (6, 7))]
SB_LATER = {1: 0, 2: 0, 4: 3, 5: 3}
CA_BANKS = [(0, (0, 1, 2, 3)), (1, (0, 1)), (1, (2, 3)), (0, (4, 5, 6, 7)), (1, (4, 5)), (1, (6, 7))]


def sb_view(tile, b):
    kb, heads = SB_BANKS[b]
    return tile[:, heads[0]:heads[-1] + 1, T:T + P] if kb else tile[:, heads[0]:heads[-1] + 1, 0:T]


def ca_view(tile, b):
    qb, heads = CA_BANKS[b]
    return tile[:, heads[0]:heads[-1] + 1, P:P + T] if qb else tile[:, heads[0]:heads[-1] + 1, 0:P]


def trunk(nc, x_in, xT_in, stream, ln_gb, mix_g, rel_band, out):
    ctx = ExitStack()
    with ctx:
        def sb(name, shape, dt=F32):
            return ctx.enter_context(nc.sbuf_tensor(name, shape, dt))

        def sem(name):
            return ctx.enter_context(nc.semaphore(name))

        raw = sb("raw", [P, 3, UW])
        w_hi = sb("w_hi", [P, 3, UW], F32R)
        w_lo = sb("w_lo", [P, 3, UW], F32R)
        xT_hi = sb("xT_hi", [P, KC, T], F32R)
        xT_lo = sb("xT_lo", [P, KC, T], F32R)
        xn = sb("xn", [P, 2, D])
        xa = sb("xa", [P, 2, D])
        sg = sb("sg", [P, 512])
        hf = sb("hf", [P, 512])
        h_hi = sb("h_hi", [P, 2, T], F32R)
        h_lo = sb("h_lo", [P, 2, T], F32R)
        hl_hi = sb("hl_hi", [P, 2, T], F32R)
        hl_lo = sb("hl_lo", [P, 2, T], F32R)
        lnp = sb("lnp", [P, 2, D])
        mixg = sb("mixg", [P, KC])
        band = sb("band", [P, HEADS, T])
        qT = sb("qT", [P, 8, T])
        kpad = sb("kpad", [P, 16, T])
        v = sb("v", [P, 2, D])
        ez = sb("ez", [P, 2, 512])
        sp_t = sb("sp_t", [P, HEADS, T + P])
        pr_t = sb("pr_t", [P, HEADS, T + P])
        table = sb("table", [P, 5, P])
        ident, neg_tri, neg_one, flip, head_mean = (table[:, i, :] for i in range(5))
        eps = sb("eps", [P, 2])
        stats = sb("stats", [P, 2, 2, 6])
        mv = sb("mv", [P, 2, 2])
        lt = sb("lt", [P, 2, 5])
        mx = sb("mx", [P, 16])
        nmx = sb("nmx", [P, 16])
        se = sb("se", [P, 16])
        rinv = sb("rinv", [P, 16])

        bank = [ctx.enter_context(nc.psum_tensor(f"bank{i}", [P, 512], F32)) for i in range(8)]
        Y = [[bank[4], bank[5]], [bank[6], bank[7]]]
        Z = [bank[2], bank[3]]
        refine = [sg, hf]
        SS = [bank[2], bank[3]]
        O = [[bank[4], bank[5]], [bank[0], bank[1]]]

        raw_ready = [sem(f"raw_ready{s}") for s in range(3)]
        half_ready = sem("half_ready")
        hi_ready = sem("hi_ready")
        lo_ready = sem("lo_ready")
        unit_used = sem("unit_used")
        x_loaded = sem("x_loaded")
        xT_loaded = [sem(f"xT_loaded{half}") for half in range(2)]
        first_hi = sem("first_hi")
        first_lo = sem("first_lo")
        consts = sem("consts")
        kzero = sem("kzero")
        pool_steps = sem("pool_steps")
        dve_steps = sem("dve_steps")
        xn_done = sem("xn_done")
        xa_done = sem("xa_done")
        xt_done = sem("xt_done")
        xhi_done = sem("xhi_done")
        xlo_done = sem("xlo_done")
        y_done = sem("y_done")
        rstd_done = sem("rstd_done")
        silu_done = sem("silu_done")
        hf_done = sem("hf_done")
        hhi_done = sem("hhi_done")
        hlo_done = sem("hlo_done")
        lnp_ready = sem("lnp_ready")
        att_par = sem("att_par")
        band_ready = sem("band_ready")
        band_mm = sem("band_mm")
        band_turned = sem("band_turned")
        ln_step = sem("ln_step")
        lnv_done = sem("lnv_done")
        unit_evac = sem("unit_evac")
        z_done = sem("z_done")
        az_done = sem("az_done")
        ez_done = sem("ez_done")
        lz_done = sem("lz_done")
        sp_done = sem("sp_done")
        spm_done = sem("spm_done")
        c_done = sem("c_done")
        w_done = sem("w_done")
        wm_done = sem("wm_done")
        t_done = sem("t_done")
        sa_done = sem("sa_done")
        mx_done = sem("mx_done")
        nm_done = sem("nm_done")
        p_done = sem("p_done")
        x_done = sem("x_done")
        pt_done = sem("pt_done")
        rinv_done = sem("rinv_done")
        pn_done = sem("pn_done")
        o_done = sem("o_done")
        sq_done = sem("sq_done")
        ss_done = sem("ss_done")
        lnr_done = sem("lnr_done")
        rr_done = sem("rr_done")
        rsq_done = sem("rsq_done")
        newton = sem("newton")
        gain_ready = sem("gain_ready")
        mix_done = sem("mix_done")
        mhi_done = sem("mhi_done")
        mlo_done = sem("mlo_done")
        stored = sem("stored")

        def used(l, rel):
            return l * UNITS + (rel + 4)

        def split(l, rel):
            return l * UNITS + (rel + 4)

        def flat(tile):
            return tile[:, :, :].rearrange("p a b -> p (a b)")

        def by_head(psum, heads):
            return psum[:, :].rearrange("p (h s) -> p h s", h=len(heads))

        def it(l, f, j):
            return l * (2 * FP) + (f * FP) + j

        def phase(l, p):
            return l * 3 + p

        HALVES = [slice(0, UW // 2), slice(UW // 2, UW)]

        def loaded(l, slot, filled):
            return l * (16 * PER_LAYER[slot]) + 16 * (filled + 1)

        block = ctx.enter_context(nc.Block())

        @block.sync
        def _(sp):
            def load(slot, n, back=3, source=None):
                sp.wait_ge(lo_ready, n + (4 - back))
                n = n if source is None else source
                if slot == 0:
                    for c, ready in zip(HALVES, (half_ready, raw_ready[0])):
                        sp.dma_start(raw[:, 0, c], stream[n][:, c]).then_inc(ready, 16)
                else:
                    sp.dma_start(raw[:, slot, :], stream[n]).then_inc(raw_ready[slot], 16)

            sp.dma_start(qT[:, 0:4, :], xT_in[:, 0:4, :]).then_inc(xT_loaded[0], 16)
            sp.sem_inc(lo_ready, 3)
            with sp.Fori(0, DEPTH) as l:
                with sp.Fori(0, (FFN_UNITS + WIN_UNITS) // 3) as i:
                    for s in range(3):
                        load(s, l * UNITS + i * 3 + s)
                for a in range(WOUT_UNITS):
                    rel = ATT0 + WIN_UNITS + a
                    load(SLOT[rel], l * UNITS + rel, back=2 if a == 0 else 3)
                for s in range(3):
                    load(s, l * UNITS + FFN_BASE[1] + s, back=2 if s == 1 else 3)
                with sp.Fori(1, FFN_UNITS // 3) as i:
                    for s in range(3):
                        load(s, l * UNITS + FFN_BASE[1] + i * 3 + s)
            load(0, DEPTH * UNITS, source=DEPTH * UNITS - 1)
            for tb in range(2):
                sp.wait_ge(xn_done, 4 * 3 * DEPTH + 2 * (tb + 1))
                sp.dma_start(out[tb * P:(tb + 1) * P, :], xn[:, tb, :]).then_inc(stored, 16)
            sp.wait_ge(stored, 32)

        @block.gpsimd
        def _(pool):
            nc.gpsimd.memset(ident, 0.0).then_inc(consts, 1)
            nc.gpsimd.memset(neg_tri, -1.0).then_inc(consts, 1)
            nc.gpsimd.memset(neg_one, -1.0).then_inc(consts, 1)
            nc.gpsimd.memset(flip, 0.0).then_inc(consts, 1)
            nc.gpsimd.memset(eps[:, 0:1], LN_EPS).then_inc(consts, 1)
            nc.gpsimd.memset(eps[:, 1:2], RMS_EPS).then_inc(consts, 1)
            nc.gpsimd.memset(head_mean, 0.0).then_inc(consts, 1)
            pool.wait_ge(consts, 7)
            nc.gpsimd.affine_select(out=ident, in_=ident, compare_op=ALU.not_equal, fill=1.0,
                                    base=0, pattern=[[-1, P]], channel_multiplier=1).then_inc(consts, 1)
            nc.gpsimd.affine_select(out=neg_tri, in_=neg_tri, compare_op=ALU.is_ge, fill=0.0,
                                    base=0, pattern=[[-1, P]], channel_multiplier=1).then_inc(consts, 1)
            nc.gpsimd.affine_select(out=flip, in_=flip, compare_op=ALU.not_equal, fill=1.0,
                                    base=1 - P, pattern=[[1, P]], channel_multiplier=1).then_inc(consts, 1)
            pool.wait_ge(consts, 10)
            nc.gpsimd.memset(head_mean[0:HD, 0:HD], 1.0 / HD).then_inc(consts, 1)
            pool.wait_ge(consts, 11)
            nc.gpsimd.memset(head_mean[HD:P, HD:P], 1.0 / HD).then_inc(consts, 1)
            pool.wait_ge(consts, 12)
            nc.gpsimd.memset(kpad[:, :, :], 0.0).then_inc(kzero, 1)

            def load_lnp(n):
                pool.dma_start(lnp[:, :, :], ln_gb[n].partition_broadcast(P)).then_inc(lnp_ready, 16)

            def wait_alone(semaphore, value):
                pool.wait_ge(semaphore, value)
                pool.sem_inc(pool_steps, 1)

            def scale_x(l, p):
                for tb in range(2):
                    wait_alone(xn_done, phase(l, p) * 4 + (2 * tb + 2))
                    nc.gpsimd.tensor_scalar(xa[:, tb, :], xn[:, tb, :], ALPHA, None, ALU.mult).then_inc(xa_done, 1)

            def causal(tiles, b, done):
                view = sb_view(tiles, b)[:, :, 0:P]
                nc.gpsimd.affine_select(out=view, in_=view, compare_op=ALU.is_gt, fill=0.0, base=0,
                                        pattern=[[0, len(SB_BANKS[b][1])], [1, P]],
                                        channel_multiplier=-1).then_inc(done, 1)

            pool.wait_ge(raw_ready[2], 16)
            pool.dma_start(xn[:, :, :], x_in.rearrange("(b p) d -> p b d", p=P)).then_inc(x_loaded, 16)
            pool.wait_ge(x_loaded, 16)
            pool.sem_inc(xn_done, 4)
            with pool.Fori(0, DEPTH) as l:
                scale_x(l, 0)
                load_lnp(l * 3)
                pool.dma_start(mixg[:, :], mix_g[l]).then_inc(att_par, 16)
                src = bass.AP(rel_band.tensor, l * (HEADS * BAND), [[1, P], [BAND, HEADS], [1, T]])
                pool.dma_start(flat(sp_t)[:, 0:HEADS * T].rearrange("p (h s) -> p h s", h=HEADS), src).then_inc(att_par, 16)
                wait_alone(att_par, (l + 1) * 32)
                nc.gpsimd.tensor_scalar(mixg[:, :], mixg[:, :], -0.5, None, ALU.mult).then_inc(gain_ready, 1)
                wait_alone(band_turned, (l + 1) * 4)
                nc.gpsimd.memset(band[0:64, :, 192:256], NEG).then_inc(band_ready, 1)
                scale_x(l, 1)
                load_lnp(l * 3 + 1)
                for b in range(7):
                    if b < 6:
                        wait_alone(sp_done, l * 6 + (b + 1))
                        causal(sp_t, b, spm_done)
                    if b > 0:
                        wait_alone(w_done, l * 6 + b)
                        causal(pr_t, b - 1, wm_done)
                scale_x(l, 2)
                load_lnp(l * 3 + 2)

        @block.scalar
        def _(act):
            act.dma_start(qT[:, 4:8, :], xT_in[:, 4:8, :]).then_inc(xT_loaded[1], 16)
            nc.scalar.preload_act_table(ACT.Silu)
            act.sem_inc(unit_used, 3)

            def split_hi(l, rel, slot, filled):
                act.wait_ge(raw_ready[slot], loaded(l, slot, filled))
                if slot == 0:
                    act.wait_ge(half_ready, loaded(l, slot, filled))
                act.wait_ge(unit_used, used(l, rel - 3))
                nc.scalar.activation(w_hi[:, slot, :], raw[:, slot, :], ACT.Copy).then_inc(hi_ready, 1)

            def split_first_hi(l, rel, filled):
                act.wait_ge(unit_used, used(l, rel - 3))
                for c, ready, done in zip(HALVES, (half_ready, raw_ready[0]), (first_hi, hi_ready)):
                    act.wait_ge(ready, loaded(l, 0, filled))
                    nc.scalar.activation(w_hi[:, 0, c], raw[:, 0, c], ACT.Copy).then_inc(done, 1)

            def split_hi_at(l, rel):
                if rel == ATT0 + WIN_UNITS:
                    act.wait_ge(unit_used, used(l, rel - 2))
                split_hi(l, rel, SLOT[rel], FILLED[rel])

            def x_hi(count, tbs=(0, 1)):
                for g in [2 * tb + half for tb in tbs for half in range(2)]:
                    tb, half = divmod(g, 2)
                    act.wait_ge(xt_done, (count - 1) * 4 + (g + 1))
                    nc.scalar.activation(xT_hi[:, 4 * half:4 * half + 4, tb * P:(tb + 1) * P],
                                         bank[g][:, :].rearrange("p (c t) -> p c t", c=4),
                                         ACT.Copy).then_inc(xhi_done, 1)

            def rstd(l, p, tb):
                n = phase(l, p) * 2 + tb
                act.wait_ge(ln_step, n * LN_STEPS + LN_VARIANCE)
                nc.scalar.activation(lt[:, tb, 0:1], mv[:, tb, 1:2], ACT.Ln, bias=eps[:, 0:1]).then_inc(lnv_done, 1)
                act.wait_ge(lnv_done, n + 1)
                nc.scalar.activation(lt[:, tb, 1:2], lt[:, tb, 0:1], ACT.Exp, scale=-0.5).then_inc(rstd_done, 1)

            def after_ln(l, p):
                for tb in range(2):
                    rstd(l, p, tb)
                    if tb == 1:
                        nc.scalar.preload_act_table(ACT.Silu)
                    x_hi(phase(l, p + 1), (tb,))

            def ffn(l, f):
                base = FFN_BASE[f]
                first = FILLED[base:base + 3]

                def silu(j, rel):
                    act.wait_ge(unit_used, used(l, base + rel))
                    nc.scalar.activation(sg[:, :], bank[0][:, :], ACT.Silu).then_inc(silu_done, 1)

                if f == 1:
                    act.wait_ge(unit_used, used(l, base - 1))
                split_hi(l, base + 1, 1, first[1])
                split_hi(l, base + 2, 2, first[2])
                silu(0, 0)
                split_hi(l, base + 3, 0, first[0] + 1)

                def h_high(j, hi):
                    act.wait_ge(hf_done, it(l, f, j) + 1)
                    nc.scalar.activation(hi[:, :, :], hf[:, :].rearrange("p (c t) -> p c t", c=2),
                                         ACT.Copy).then_inc(hhi_done, 1)

                def step(j):
                    act.wait_ge(unit_used, used(l, base + 3 * j + 1))
                    h_high(j, h_hi)
                    split_hi(l, base + 3 * j + 4, 1, first[1] + 1 + j)
                    split_hi(l, base + 3 * j + 5, 2, first[2] + 1 + j)
                    silu(j + 1, 3 * j + 2)

                with act.Fori(0, FP - 2) as j:
                    step(j)
                    split_hi(l, base + 3 * j + 6, 0, first[0] + 2 + j)
                step(FP - 2)
                h_high(FP - 1, hl_hi)
                split_first_hi(l, base + FFN_UNITS, first[0] + FP)
                nc.scalar.preload_act_table_set("natural_log_exp_and_others")

            def band_out(l, i):
                act.wait_ge(band_mm, l * 4 + (i + 1))
                nc.scalar.activation(band[:, 2 * i:2 * i + 2, :],
                                     bank[2 + i % 2][:, :].rearrange("p (h s) -> p h s", h=2),
                                     ACT.Copy).then_inc(band_turned, 1)

            def evacuate(l, a):
                kind, part, half = W_IN[a]
                two = bank[a % 2][:, :].rearrange("p (c t) -> p c t", c=2)
                act.wait_ge(unit_used, used(l, ATT0 + a))
                if kind == "q":
                    nc.scalar.activation(qT[:, 4 * part + 2 * half:4 * part + 2 * half + 2, :], two,
                                         ACT.Copy, scale=QSCALE).then_inc(unit_evac, 1)
                elif kind == "k":
                    h0 = 8 * part + 4 * half
                    nc.scalar.activation(kpad[0:64, h0:h0 + 4:2, :], two[0:64], ACT.Copy)
                    nc.scalar.activation(kpad[64:128, h0 + 1:h0 + 4:2, :], two[64:128],
                                         ACT.Copy).then_inc(unit_evac, 1)
                else:
                    c0 = 512 * part + 256 * half
                    nc.scalar.activation(v[:, :, c0:c0 + 256], two, ACT.Copy).then_inc(unit_evac, 1)

            def log_keep(l, b):
                e = ez[:, b % 2, :]
                act.wait_ge(z_done, l * 6 + (b + 1))
                if b >= 2:
                    act.wait_ge(sp_done, l * 6 + (b - 1))
                nc.scalar.activation(e, Z[b % 2][:, :], ACT.Abs).then_inc(az_done, 1)
                act.wait_ge(az_done, l * 6 + (b + 1))
                nc.scalar.activation(e, e, ACT.Exp, scale=-1.0).then_inc(ez_done, 1)
                act.wait_ge(ez_done, l * 6 + (b + 1))
                nc.scalar.activation(e, e, ACT.Ln, bias=1.0).then_inc(lz_done, 1)

            def weights(l, b):
                act.wait_ge(c_done, l * 6 + (b + 1))
                nc.scalar.activation(sb_view(pr_t, b), by_head(Z[b % 2], SB_BANKS[b][1]), ACT.Exp).then_inc(w_done, 1)

            def softmax_exp(l, b):
                qb, heads = CA_BANKS[b]
                act.wait_ge(nm_done, l * 6 + (b + 1))
                for i, h in enumerate(heads):
                    c = 8 * qb + h
                    s = ca_view(sp_t, b)[:, i, :]
                    last = nc.scalar.activation(s, s,
                                                ACT.Exp, bias=nmx[:, c:c + 1], accum_out=se[:, c:c + 1])
                last.then_inc(p_done, 1)

            def square(l, part, i):
                g = l * 4 + (2 * part + i)
                act.wait_ge(o_done, g + 1)
                if part == 1:
                    act.wait_ge(mix_done, g - 1)
                nc.scalar.activation(ez[:, i, :], O[part][i][:, :], ACT.Square).then_inc(sq_done, 1)

            def head_rstd(l, part, i):
                g = l * 4 + (2 * part + i)
                act.wait_ge(ss_done, g + 1)
                nc.scalar.activation(ez[:, i, :], SS[i][:, :], ACT.Ln, bias=eps[:, 1:2]).then_inc(lnr_done, 1)
                act.wait_ge(lnr_done, g + 1)
                nc.scalar.activation(ez[:, i, :], ez[:, i, :], ACT.Exp, scale=-0.5).then_inc(rr_done, 1)
                act.wait_ge(rr_done, g + 1)
                nc.scalar.activation(refine[i][:, :], ez[:, i, :], ACT.Square).then_inc(rsq_done, 1)

            def mixed_hi(l, part):
                act.wait_ge(unit_used, used(l, ATT0 + WIN_UNITS - 1))
                for i in range(2):
                    act.wait_ge(mix_done, l * 4 + (2 * part + i + 1))
                    c = slice(4 * part + 2 * i, 4 * part + 2 * i + 2)
                    nc.scalar.activation(xT_hi[:, c, :], qT[:, c, :], ACT.Copy).then_inc(mhi_done, 1)

            def attention(l):
                act.wait_ge(kzero, 1)
                split_hi_at(l, ATT0 + 1)
                split_hi_at(l, ATT0 + 2)
                for a in range(3):
                    evacuate(l, a)
                    split_hi_at(l, ATT0 + a + 3)
                evacuate(l, 3)
                log_keep(l, 0)
                split_hi_at(l, ATT0 + 6)
                for b in range(5):
                    evacuate(l, 4 + b)
                    log_keep(l, b + 1)
                    weights(l, b)
                    if b < 4:
                        split_hi_at(l, ATT0 + 7 + b)
                softmax_exp(l, 0)
                softmax_exp(l, 1)
                split_hi_at(l, ATT0 + 11)
                evacuate(l, 9)
                weights(l, 5)
                softmax_exp(l, 2)
                softmax_exp(l, 3)
                square(l, 0, 0)
                square(l, 0, 1)
                softmax_exp(l, 4)
                evacuate(l, 10)
                head_rstd(l, 0, 0)
                head_rstd(l, 0, 1)
                softmax_exp(l, 5)
                split_hi_at(l, ATT0 + 12)
                evacuate(l, 11)
                mixed_hi(l, 0)
                split_hi_at(l, ATT0 + 13)
                square(l, 1, 0)
                square(l, 1, 1)
                split_hi_at(l, ATT0 + 14)
                head_rstd(l, 1, 0)
                head_rstd(l, 1, 1)
                split_hi_at(l, ATT0 + 15)
                mixed_hi(l, 1)
                split_first_hi(l, FFN_BASE[1], FILLED[FFN_BASE[1]])

            for half, c in enumerate(HALVES):
                part = slice(4 * half, 4 * half + 4)
                act.wait_ge(xT_loaded[half], 16)
                nc.scalar.activation(xT_hi[:, part, :], qT[:, part, :], ACT.Copy).then_inc(xhi_done, (3, 1)[half])
                act.wait_ge((half_ready, raw_ready[0])[half], 16)
                nc.scalar.activation(w_hi[:, 0, c], raw[:, 0, c], ACT.Copy).then_inc((first_hi, hi_ready)[half], 1)
            act.wait_ge(consts, 12)
            with act.Fori(0, DEPTH) as l:
                ffn(l, 0)
                rstd(l, 0, 0)
                x_hi(phase(l, 1), (0,))
                band_out(l, 0)
                band_out(l, 1)
                rstd(l, 0, 1)
                band_out(l, 2)
                band_out(l, 3)
                x_hi(phase(l, 1), (1,))
                attention(l)
                after_ln(l, 1)
                ffn(l, 1)
                after_ln(l, 2)

        @block.vector
        def _(dve):
            def split_lo(l, rel, slot):
                dve.wait_ge(hi_ready, l * UNITS + (rel + 1))
                nc.vector.tensor_tensor(w_lo[:, slot, :], raw[:, slot, :], w_hi[:, slot, :].bitcast(F32),
                                        ALU.subtract).then_inc(lo_ready, 1)

            def split_half_lo(half):
                c = HALVES[half]
                nc.vector.tensor_tensor(w_lo[:, 0, c], raw[:, 0, c], w_hi[:, 0, c].bitcast(F32),
                                        ALU.subtract).then_inc((first_lo, lo_ready)[half], 1)

            def split_first_lo(l, p, rel):
                dve.wait_ge(first_hi, phase(l, p) + 1)
                split_half_lo(0)
                dve.wait_ge(hi_ready, l * UNITS + (rel + 1))
                split_half_lo(1)

            def x_lo(count):
                for g in range(4):
                    tb, half = divmod(g, 2)
                    dve.wait_ge(xhi_done, count * 4 + (g + 1))
                    part = slice(4 * half, 4 * half + 4), slice(tb * P, (tb + 1) * P)
                    nc.vector.tensor_tensor(xT_lo[:, part[0], part[1]],
                                            bank[g][:, :].rearrange("p (c t) -> p c t", c=4),
                                            xT_hi[:, part[0], part[1]].bitcast(F32),
                                            ALU.subtract).then_inc(xlo_done, 1)

            def layer_norm(l, p):
                scale = 1.0 if p == 1 else 0.5
                dve.wait_ge(lnp_ready, phase(l, p) * 16 + 16)
                for tb in range(2):
                    n = phase(l, p) * 2 + tb
                    k = [0]

                    def done(ins):
                        k[0] += 1
                        ins.then_inc(ln_step, 1)

                    def after(count):
                        dve.wait_ge(ln_step, n * LN_STEPS + count)

                    halves = [slice(512 * half, 512 * half + 512) for half in range(2)]
                    dve.wait_ge(xa_done, n + 1)
                    for half, cols in enumerate(halves):
                        dve.wait_ge(y_done, n * 2 + (half + 1))
                        done(nc.vector.scalar_tensor_tensor(out=xn[:, tb, cols], in0=Y[tb][half][:, :],
                                                            scalar=scale, in1=xa[:, tb, cols],
                                                            op0=ALU.mult, op1=ALU.add))
                        after(k[0])
                        done(nc.vector.bn_stats(stats[:, tb, half, :], xn[:, tb, cols]))
                    after(k[0])
                    dve.sem_inc(dve_steps, 1)
                    done(nc.vector.bn_aggr(mv[:, tb, :], stats[:, tb, :, :].rearrange("p a b -> p (a b)")))
                    assert k[0] == LN_VARIANCE
                    after(k[0])
                    for cols in halves:
                        done(nc.vector.scalar_tensor_tensor(out=xn[:, tb, cols], in0=xn[:, tb, cols],
                                                            scalar=mv[:, tb, 0:1], in1=lnp[:, 0, cols],
                                                            op0=ALU.subtract, op1=ALU.mult))
                    done(nc.vector.tensor_scalar(lt[:, tb, 2:3], mv[:, tb, 1:2], LN_EPS, -0.5, ALU.add,
                                                 ALU.mult))
                    after(k[0])
                    dve.wait_ge(rstd_done, n + 1)
                    y = lt[:, tb, 1:2]
                    done(nc.vector.tensor_scalar(lt[:, tb, 3:4], y, y, lt[:, tb, 2:3], ALU.mult, ALU.mult))
                    after(k[0])
                    done(nc.vector.tensor_scalar(lt[:, tb, 4:5], lt[:, tb, 3:4], 1.5, y, ALU.add, ALU.mult))
                    assert k[0] == LN_STEPS
                    after(k[0])
                    for cols in halves:
                        nc.vector.scalar_tensor_tensor(out=xn[:, tb, cols], in0=xn[:, tb, cols],
                                                       scalar=lt[:, tb, 4:5], in1=lnp[:, 1, cols],
                                                       op0=ALU.mult, op1=ALU.add).then_inc(xn_done, 1)

            def ffn(l, f):
                base = FFN_BASE[f]

                def gated(step, rel, first=False):
                    if not first:
                        dve.wait_ge(hlo_done, step)
                    dve.wait_ge(silu_done, step + 1)
                    dve.wait_ge(unit_used, used(l, base + rel))
                    nc.vector.tensor_tensor(hf[:, :], sg[:, :], bank[1][:, :], ALU.mult).then_inc(hf_done, 1)

                def h_low(step, hi, lo):
                    dve.wait_ge(hhi_done, step + 1)
                    nc.vector.tensor_tensor(lo[:, :, :], hf[:, :].rearrange("p (c t) -> p c t", c=2),
                                            hi[:, :, :].bitcast(F32), ALU.subtract).then_inc(hlo_done, 1)

                split_lo(l, base + 1, 1)
                split_lo(l, base + 2, 2)
                gated(it(l, f, 0), 1, first=True)
                split_lo(l, base + 3, 0)

                def step(j):
                    h_low(it(l, f, j), h_hi, h_lo)
                    split_lo(l, base + 3 * j + 4, 1)
                    split_lo(l, base + 3 * j + 5, 2)
                    gated(it(l, f, j) + 1, 3 * j + 3)

                with dve.Fori(0, FP - 2) as j:
                    step(j)
                    split_lo(l, base + 3 * j + 6, 0)
                step(FP - 2)
                h_low(it(l, f, FP - 1), hl_hi, hl_lo)
                split_first_lo(l, 2 * f + 1, base + FFN_UNITS)

            def split_lo_at(l, rel):
                split_lo(l, rel, SLOT[rel])

            def softplus(l, b):
                dve.wait_ge(lz_done, l * 6 + (b + 1))
                nc.vector.scalar_tensor_tensor(out=sb_view(sp_t, b), in0=by_head(Z[b % 2], SB_BANKS[b][1]),
                                               scalar=0.0, in1=by_head(ez[:, b % 2, :], SB_BANKS[b][1]),
                                               op0=ALU.max, op1=ALU.add).then_inc(sp_done, 1)

            def scores(l, b):
                qb, heads = CA_BANKS[b]
                n, m = len(heads), 512 // len(heads)
                s = ca_view(sp_t, b)
                c = slice(8 * qb + heads[0], 8 * qb + heads[0] + n)
                dve.wait_ge(t_done, l * 6 + (b + 1))
                nc.vector.tensor_tensor(s, by_head(bank[6], heads),
                                        band[:, heads[0]:heads[0] + n, T - m:T], ALU.add).then_inc(sa_done, 1)
                dve.wait_ge(sa_done, l * 6 + (b + 1))
                nc.vector.tensor_reduce(mx[:, c], s, AX_X, ALU.max).then_inc(mx_done, 1)
                dve.wait_ge(mx_done, l * 6 + (b + 1))
                nc.vector.tensor_scalar(nmx[:, c], mx[:, c], -1.0, None, ALU.mult).then_inc(nm_done, 1)

            def normalise(l, b):
                qb, heads = CA_BANKS[b]
                c = slice(8 * qb + heads[0], 8 * qb + heads[-1] + 1)
                s = ca_view(sp_t, b)
                dve.wait_ge(p_done, l * 6 + (b + 1))
                nc.vector.reciprocal(rinv[:, c], se[:, c]).then_inc(rinv_done, 1)
                dve.wait_ge(rinv_done, l * 6 + (b + 1))
                r = rinv[:, c].unsqueeze(2).to_broadcast([P, len(heads), 512 // len(heads)])
                nc.vector.tensor_tensor(s, s, r, ALU.mult).then_inc(pn_done, 1)

            def turned(l, b):
                dve.wait_ge(x_done, l * 6 + (b + 1))
                nc.vector.tensor_copy(ca_view(sp_t, b), by_head(bank[7], CA_BANKS[b][1])).then_inc(pt_done, 1)

            def mix(l, part, i):
                g = l * 4 + (2 * part + i)
                y2, y = refine[i][:, :], ez[:, i, :]
                if part == 0 and i == 0:
                    dve.wait_ge(gain_ready, l + 1)
                dve.wait_ge(rsq_done, g + 1)
                nc.vector.scalar_tensor_tensor(out=y2, in0=SS[i][:, :], scalar=RMS_EPS, in1=y2,
                                               op0=ALU.add, op1=ALU.mult).then_inc(newton, 1)
                dve.wait_ge(newton, 2 * g + 1)
                nc.vector.scalar_tensor_tensor(out=y, in0=y2, scalar=-3.0, in1=y,
                                               op0=ALU.add, op1=ALU.mult).then_inc(newton, 1)
                dve.wait_ge(newton, 2 * g + 2)
                for k in range(2):
                    c = 4 * part + 2 * i + k
                    last = nc.vector.scalar_tensor_tensor(
                        out=qT[:, c, :], in0=O[part][i][:, k * T:(k + 1) * T], scalar=mixg[:, c:c + 1],
                        in1=ez[:, i, k * T:(k + 1) * T], op0=ALU.mult, op1=ALU.mult)
                last.then_inc(mix_done, 1)

            def mixed_lo(l, part):
                for i in range(2):
                    dve.wait_ge(mhi_done, l * 4 + (2 * part + i + 1))
                    c = slice(4 * part + 2 * i, 4 * part + 2 * i + 2)
                    nc.vector.tensor_tensor(xT_lo[:, c, :], qT[:, c, :], xT_hi[:, c, :].bitcast(F32),
                                            ALU.subtract).then_inc(mlo_done, 1)

            def attention(l):
                for rel in range(1, 6):
                    split_lo_at(l, ATT0 + rel)
                softplus(l, 0)
                split_lo_at(l, ATT0 + 6)
                dve.wait_ge(band_ready, l + 1)
                for b in range(5):
                    if b == 4:
                        scores(l, 0)
                    softplus(l, b + 1)
                    if b < 4:
                        split_lo_at(l, ATT0 + 7 + b)
                scores(l, 1)
                normalise(l, 0)
                normalise(l, 1)
                turned(l, 0)
                scores(l, 2)
                split_lo_at(l, ATT0 + 11)
                turned(l, 1)
                scores(l, 3)
                normalise(l, 2)
                normalise(l, 3)
                turned(l, 2)
                scores(l, 4)
                normalise(l, 4)
                turned(l, 3)
                scores(l, 5)
                mix(l, 0, 0)
                turned(l, 4)
                normalise(l, 5)
                mix(l, 0, 1)
                turned(l, 5)
                split_lo_at(l, ATT0 + 12)
                mixed_lo(l, 0)
                split_lo_at(l, ATT0 + 13)
                split_lo_at(l, ATT0 + 14)
                mix(l, 1, 0)
                mix(l, 1, 1)
                mixed_lo(l, 1)
                split_lo_at(l, ATT0 + 15)
                split_first_lo(l, 2, FFN_BASE[1])

            for half in range(2):
                part = slice(4 * half, 4 * half + 4)
                dve.wait_ge(xhi_done, (3, 4)[half])
                nc.vector.tensor_tensor(xT_lo[:, part, :], qT[:, part, :], xT_hi[:, part, :].bitcast(F32),
                                        ALU.subtract).then_inc(xlo_done, (3, 1)[half])
                dve.wait_ge((first_hi, hi_ready)[half], 1)
                split_half_lo(half)
            with dve.Fori(0, DEPTH) as l:
                ffn(l, 0)
                layer_norm(l, 0)
                x_lo(phase(l, 1))
                attention(l)
                layer_norm(l, 1)
                x_lo(phase(l, 2))
                ffn(l, 1)
                layer_norm(l, 2)
                x_lo(phase(l, 3))

        @block.tensor
        def _(pe):
            def three(o, w, x, start, stop):
                nc.tensor.matmul(o, w[0], x[0], start=start, stop=False)
                nc.tensor.matmul(o, w[0], x[1], start=False, stop=False)
                return nc.tensor.matmul(o, w[1], x[0], start=False, stop=stop)

            def columns(l, rel, slot, out_bank, halves=(0, 1)):
                pe.wait_ge(lo_ready, split(l, rel))
                for c in halves:
                    for kc in range(KC):
                        w = slice(kc * 256 + c * P, kc * 256 + (c + 1) * P)
                        last = three(out_bank[:, c * T:(c + 1) * T], (w_hi[:, slot, w], w_lo[:, slot, w]),
                                     (xT_hi[:, kc, :], xT_lo[:, kc, :]), kc == 0, kc == KC - 1)
                if halves[-1] == 1:
                    last.then_inc(unit_used, 1)

            def rows(l, rel, slot, out_bank, halves=(0, 1)):
                pe.wait_ge(lo_ready, split(l, rel))
                for tb in halves:
                    for kc in range(KC):
                        w = slice(kc * 256, (kc + 1) * 256)
                        t = slice(tb * P, (tb + 1) * P)
                        last = three(out_bank[:, tb * 256:(tb + 1) * 256], (xT_hi[:, kc, t], xT_lo[:, kc, t]),
                                     (w_hi[:, slot, w], w_lo[:, slot, w]), kc == 0, kc == KC - 1)
                if halves[-1] == 1:
                    last.then_inc(unit_used, 1)

            def down(slot, hi, lo, c0, tbs, start=False, stop=False, halves=(0, 1)):
                for tb in tbs:
                    for half in halves:
                        for c in range(2):
                            w = slice(c * D + half * 512, c * D + half * 512 + 512)
                            t = slice(tb * P, (tb + 1) * P)
                            last = three(Y[tb][half][:, :], (hi[:, c0 + c, t], lo[:, c0 + c, t]),
                                         (w_hi[:, slot, w], w_lo[:, slot, w]),
                                         start and c == 0, stop and c == 1)
                return last

            def turn_x(tb, count, band_turned_by=None):
                if band_turned_by is not None:
                    pe.wait_ge(band_turned, band_turned_by)
                for half in range(2):
                    pe.wait_ge(xn_done, count * 4 + (2 * tb + half + 1))
                    for q in range(4):
                        c = (4 * half + q) * P
                        last = nc.tensor.transpose(bank[2 * tb + half][:, q * P:(q + 1) * P],
                                                   xn[:, tb, c:c + P], ident)
                    last.then_inc(xt_done, 1)

            def turn_band(l):
                pe.wait_ge(att_par, (l + 1) * 32)
                for i in range(4):
                    if i >= 2:
                        pe.wait_ge(band_turned, l * 4 + (i - 1))
                    nc.tensor.matmul(bank[2 + i % 2][:, :], flip, flat(sp_t)[:, i * 512:(i + 1) * 512], start=True,
                                     stop=True).then_inc(band_mm, 1)

            def keep_warm(count):
                for i in range(count):
                    nc.tensor.matmul(bank[3][:, :], ident, flat(table)[:, 0:512],
                                     start=True, stop=True)

            def first_columns(l, rel, count):
                for kh in range(2):
                    if kh == 0:
                        pe.wait_ge(first_lo, count + 1)
                    else:
                        pe.wait_ge(lo_ready, split(l, rel))
                    pe.wait_ge(xlo_done, count * 4 + (3 + kh))
                    for c in range(2):
                        for kc in range(4 * kh, 4 * kh + 4):
                            w = slice(kc * 256 + c * P, kc * 256 + (c + 1) * P)
                            o = bank[0][:, c * T:(c + 1) * T]
                            plain(o, w_hi[:, 0, w], xT_hi[:, kc, :], start=kc == 0 and c == 0)
                            plain(o, w_hi[:, 0, w], xT_lo[:, kc, :])
                            last = plain(o, w_lo[:, 0, w], xT_hi[:, kc, :], stop=kc == KC - 1)
                last.then_inc(unit_used, 1)

            def plain(o, w, x, start=False, stop=False):
                return nc.tensor.matmul(o, w, x, start=start, stop=stop, skip_group_check=True)

            def last_used(n, units):
                pe.wait_ge(y_done, n * 4 + 4)
                pe.sem_inc(unit_used, units)

            def ffn(l, f, count):
                base = FFN_BASE[f]
                first_columns(l, base, count)
                columns(l, base + 1, 1, bank[1])

                def gate_up(j):
                    pe.wait_ge(silu_done, it(l, f, j) + 1)
                    columns(l, base + 3 * j + 2, 2, bank[0])
                    pe.wait_ge(hf_done, it(l, f, j) + 1)
                    columns(l, base + 3 * j + 3, 0, bank[1])

                def step(j, start):
                    gate_up(j)
                    pe.wait_ge(hlo_done, it(l, f, j) + 1)
                    pe.wait_ge(lo_ready, split(l, base + 3 * j + 4))
                    down(1, h_hi, h_lo, 0, (0, 1), start=start).then_inc(unit_used, 1)

                step(0, True)
                with pe.Fori(1, FP - 2) as j:
                    step(j, False)
                gate_up(FP - 2)
                pe.wait_ge(hlo_done, it(l, f, FP - 1))
                pe.wait_ge(lo_ready, split(l, base + FFN_UNITS - 2))
                for tb in range(2):
                    last = down(1, h_hi, h_lo, 0, (tb,))
                    if tb == 1:
                        last.then_inc(unit_used, 1)
                    if tb == 0:
                        pe.wait_ge(hlo_done, it(l, f, FP))
                        pe.wait_ge(lo_ready, split(l, base + FFN_UNITS - 1))
                    for half in range(2):
                        down(2, hl_hi, hl_lo, 0, (tb,), stop=True, halves=(half,)).then_inc(y_done, 1)
                last_used(phase(l, 2 * f), 1)

            def sb_scores(l, b):
                kb, heads = SB_BANKS[b]
                if b == 0:
                    pe.wait_ge(unit_evac, l * WIN_UNITS + 4)
                if b >= 2:
                    pe.wait_ge(w_done, l * 6 + (b - 1))
                m = 512 // len(heads)
                for i, h in enumerate(heads):
                    last = plain(Z[b % 2][:, i * m:(i + 1) * m], kpad[:, h, kb * P:(kb + 1) * P],
                                 qT[:, h // 2, T - m:T], start=i == 0)
                last.then_inc(z_done, 1)

            def sb_sums(l, b):
                kb, heads = SB_BANKS[b]
                z = Z[b % 2]
                pe.wait_ge(spm_done, l * 6 + (b + 1))
                last = plain(z[:, :], neg_tri, sb_view(sp_t, b), stop=kb == 1)
                if kb == 0:
                    last = plain(by_head(z, heads)[:, :, P:T], neg_one, sp_t[:, heads[0]:heads[-1] + 1, T:T + P],
                                 stop=True)
                last.then_inc(c_done, 1)

            def values(l, part, i):
                w = (pr_t, sp_t)[part]
                if part == 0:
                    pe.wait_ge(wm_done, l * 6 + 3 * (i + 1))
                    pe.wait_ge(unit_evac, l * WIN_UNITS + (9 + i))
                else:
                    pe.wait_ge(pt_done, l * 6 + 3 * (i + 1))
                    pe.wait_ge(unit_evac, l * WIN_UNITS + (11 + i))
                for h in range(4 * i, 4 * i + 4):
                    rows_of = slice((h % 2) * HD, (h % 2 + 1) * HD)
                    c = (h // 2 % 2) * T
                    d = slice(512 * part + h * HD, 512 * part + (h + 1) * HD)
                    plain(O[part][i][rows_of, c:c + T], v[:, 0, d], w[:, h, 0:T], start=True)
                    last = plain(O[part][i][rows_of, c + P:c + T], v[:, 1, d], w[:, h, T:T + P], stop=True)
                last.then_inc(o_done, 1)

            def head_means(l, part):
                for i in range(2):
                    pe.wait_ge(sq_done, l * 4 + (2 * part + i + 1))
                    plain(SS[i][:, :], head_mean, ez[:, i, :], start=True, stop=True).then_inc(ss_done, 1)

            def ca_scores(l, b):
                qb, heads = CA_BANKS[b]
                if b == 0:
                    pe.wait_ge(unit_evac, l * WIN_UNITS + 8)
                else:
                    pe.wait_ge(sa_done, l * 6 + b)
                m = 512 // len(heads)
                for i, h in enumerate(heads):
                    last = plain(bank[6][:, i * m:(i + 1) * m], qT[:, 4 + h // 2, qb * P:(qb + 1) * P],
                                 kpad[:, 8 + h, 0:m], start=True, stop=True)
                last.then_inc(t_done, 1)

            def ca_turn(l, b):
                pe.wait_ge(pn_done, l * 6 + (b + 1))
                if b > 0:
                    pe.wait_ge(pt_done, l * 6 + b)
                n = 512 // len(CA_BANKS[b][1]) // P
                for q in range(4):
                    c = (q % n) * P
                    last = nc.tensor.transpose(bank[7][:, q * P:(q + 1) * P],
                                               ca_view(sp_t, b)[:, q // n, c:c + P], ident)
                last.then_inc(x_done, 1)

            def w_in(l, a, halves=(0, 1)):
                if a >= 2 and halves[0] == 0:
                    pe.wait_ge(unit_evac, l * WIN_UNITS + (a - 1))
                f = rows if W_IN[a][0] == "v" else columns
                f(l, ATT0 + a, SLOT[ATT0 + a], bank[a % 2], halves)

            def attention(l):
                first_columns(l, ATT0, phase(l, 1))
                for a in range(1, 4):
                    w_in(l, a)
                w_in(l, 4, (0,))
                sb_scores(l, 0)
                w_in(l, 4, (1,))
                for b in range(4):
                    if b > 0:
                        w_in(l, 4 + b)
                    sb_scores(l, b + 1)
                    sb_sums(l, b)
                w_in(l, 8, (0,))
                ca_scores(l, 0)
                w_in(l, 8, (1,))
                sb_scores(l, 5)
                sb_sums(l, 4)
                ca_scores(l, 1)
                w_in(l, 9, (0,))
                ca_turn(l, 0)
                ca_scores(l, 2)
                w_in(l, 9, (1,))
                sb_sums(l, 5)
                ca_turn(l, 1)
                ca_scores(l, 3)
                w_in(l, 10, (0,))
                values(l, 0, 0)
                values(l, 0, 1)
                ca_turn(l, 2)
                ca_scores(l, 4)
                w_in(l, 10, (1,))
                head_means(l, 0)
                ca_turn(l, 3)
                ca_scores(l, 5)
                w_in(l, 11, (0,))
                ca_turn(l, 4)
                w_in(l, 11, (1,))
                ca_turn(l, 5)
                values(l, 1, 0)
                values(l, 1, 1)
                rels = [ATT0 + WIN_UNITS + i for i in range(WOUT_UNITS)]
                for i in range(2):
                    pe.wait_ge(mlo_done, l * 4 + (i + 1))
                    pe.wait_ge(lo_ready, split(l, rels[i]))
                    for tb in range(2):
                        last = down(SLOT[rels[i]], xT_hi, xT_lo, 2 * i, (tb,), start=i == 0)
                        if tb == 1:
                            last.then_inc(unit_used, 1)
                        elif i == 0:
                            head_means(l, 1)
                for tb in range(2):
                    for i in (2, 3):
                        if tb == 0:
                            pe.wait_ge(mlo_done, l * 4 + (i + 1))
                            pe.wait_ge(lo_ready, split(l, rels[i]))
                        for half in range(2):
                            last = down(SLOT[rels[i]], xT_hi, xT_lo, 2 * i, (tb,), stop=i == 3, halves=(half,))
                            if i == 3:
                                last.then_inc(y_done, 1)
                last_used(phase(l, 1), 2)

            pe.wait_ge(consts, 12)
            with pe.Fori(0, DEPTH) as l:
                ffn(l, 0, phase(l, 0))
                turn_x(0, phase(l, 1))
                turn_band(l)
                turn_x(1, phase(l, 1), (l + 1) * 4)
                attention(l)
                turn_x(0, phase(l, 2))
                keep_warm(5)
                turn_x(1, phase(l, 2))
                ffn(l, 1, phase(l, 2))
                turn_x(0, phase(l, 3))
                keep_warm(5)
                turn_x(1, phase(l, 3))


_ARGS = ["x", "ffn1_w_gate", "ffn1_w_up", "ffn1_w_down", "ln1_g", "ln1_b", "w_in", "rel_bias", "sb_out_g",
         "ca_out_g", "w_out", "ln2_g", "ln2_b", "ffn2_w_gate", "ffn2_w_up", "ffn2_w_down", "ln3_g", "ln3_b"]


def column_units(w):
    k, n = w.shape
    return w.reshape(k // P, P, n // 256, 256).transpose(2, 1, 0, 3).reshape(n // 256, P, UW)


def row_units(w):
    return w.reshape(w.shape[0] // 256, 2, P, D).transpose(0, 2, 1, 3).reshape(-1, P, UW)


def weight_stream(ins):
    units = []
    for l in range(DEPTH):
        for f in ("ffn1", "ffn2"):
            g, u = (column_units(ins[f"{f}_w_{k}"][l]) for k in ("gate", "up"))
            d = row_units(ins[f"{f}_w_down"][l])
            units += [g[0], u[0]]
            for j in range(FP - 1):
                units += [g[j + 1], u[j + 1], d[j]]
            units.append(d[FP - 1])
            if f == "ffn1":
                w = column_units(ins["w_in"][l])
                units += [w[6 * part + 2 * "qkv".index(kind) + half] for kind, part, half in W_IN]
                units += list(row_units(ins["w_out"][l]))
    return np.stack(units)


def kernel(**inputs):
    import concourse.bacc as bacc
    from concourse.bass_utils import run_bass_kernel_spmd

    ins = {k: np.asarray(inputs[k]) for k in _ARGS}
    ln = np.stack([np.stack([ins[f"ln{i}_{k}"] for k in "gb"], 1) for i in (1, 2, 3)], 1)
    ln = ln.reshape(DEPTH * 3, 2, D)
    mix = np.concatenate([ins["sb_out_g"], ins["ca_out_g"]], 1).reshape(DEPTH, KC, P).transpose(0, 2, 1)
    flipped = ins["rel_bias"][:, :, ::-1]
    rel = np.concatenate([np.repeat(flipped[:, :, :1], P - 1, axis=2), flipped], 2)
    x = ins["x"].reshape(T, D)
    arrays = {
        "x": x,
        "xT": x.reshape(T, KC, P).transpose(2, 1, 0),
        "stream": weight_stream(ins),
        "ln_gb": ln,
        "mix_g": mix,
        "rel_band": rel,
    }
    arrays = {k: np.ascontiguousarray(a) for k, a in arrays.items()}
    nc = bacc.Bacc("TRN2", target_bir_lowering=False, num_devices=1)
    args = [nc.dram_tensor(k, a.shape, F32, kind="ExternalInput").ap() for k, a in arrays.items()]
    out = nc.dram_tensor("out", (T, D), F32, kind="ExternalOutput").ap()
    trunk(nc, *args, out)
    r = run_bass_kernel_spmd(nc, [arrays], core_ids=[0])
    return r.results[0]["out"].reshape(1, T, D)
```

```python
from contextlib import ExitStack

import numpy as np

import concourse.bass as bass
from concourse import mybir

ALU = mybir.AluOpType
ACT = mybir.ActivationFunctionType
F32 = mybir.dt.float32
F32R = mybir.dt.float32r
AX_X = mybir.AxisListType.X

P = 128
D = 1024
T = 256
DEPTH = 2
F = 2816
HD = 64
HEADS = 8
MAX_REL = 128
BAND = 2 * MAX_REL + P
KC = D // P
FP = F // (2 * P)
UW = 2048
LN_EPS = 1e-5
RMS_EPS = 1e-6
ALPHA = float((2 * DEPTH) ** 0.25)
QSCALE = 1.0 / 8.0
NEG = -3.0e38

FFN_UNITS = 3 * FP
WIN_UNITS = 12
WOUT_UNITS = 4
UNITS = 2 * FFN_UNITS + WIN_UNITS + WOUT_UNITS
ATT0 = FFN_UNITS
FFN_BASE = (0, FFN_UNITS + WIN_UNITS + WOUT_UNITS)


def unit_slots():
    order = [n % 3 for n in range(FFN_UNITS)]
    order += [a % 3 for a in range(WIN_UNITS)] + [1, 0, 2, 1]
    order += [n % 3 for n in range(FFN_UNITS)]
    seen, before = [0, 0, 0], []
    for s in order:
        before.append(seen[s])
        seen[s] += 1
    return order, before, seen


LN_MEAN, LN_STEPS = 3, 8

SLOT, FILLED, PER_LAYER = unit_slots()

W_IN = [(kind, part, half) for kind, part in (("q", 0), ("k", 0), ("q", 1), ("k", 1), ("v", 0), ("v", 1))
        for half in range(2)]
SB_BANKS = [(1, (0, 1, 2, 3)), (0, (0, 1)), (0, (2, 3)), (1, (4, 5, 6, 7)), (0, (4, 5)), (0, (6, 7))]
SB_LATER = {1: 0, 2: 0, 4: 3, 5: 3}
CA_BANKS = [(0, (0, 1, 2, 3)), (1, (0, 1)), (1, (2, 3)), (0, (4, 5, 6, 7)), (1, (4, 5)), (1, (6, 7))]


def sb_view(tile, b):
    kb, heads = SB_BANKS[b]
    return tile[:, heads[0]:heads[-1] + 1, T:T + P] if kb else tile[:, heads[0]:heads[-1] + 1, 0:T]


def ca_view(tile, b):
    qb, heads = CA_BANKS[b]
    return tile[:, heads[0]:heads[-1] + 1, P:P + T] if qb else tile[:, heads[0]:heads[-1] + 1, 0:P]


def trunk(nc, x_in, xT_in, stream, ln_gb, mix_g, rel_band, out):
    ctx = ExitStack()
    with ctx:
        def sb(name, shape, dt=F32):
            return ctx.enter_context(nc.sbuf_tensor(name, shape, dt))

        def flat(tile):
            return tile[:, :, :].rearrange("p a b -> p (a b)")

        def sem(name):
            return ctx.enter_context(nc.semaphore(name))

        raw = sb("raw", [P, 3, UW])
        w_hi = sb("w_hi", [P, 3, UW], F32R)
        w_lo = sb("w_lo", [P, 3, UW], F32R)
        xT_hi = sb("xT_hi", [P, KC, T], F32R)
        xT_lo = sb("xT_lo", [P, KC, T], F32R)
        xn = sb("xn", [P, 2, D])
        centred = sb("centred", [P, 2, D])
        scratch = sb("scratch", [P, 2, 512])
        sg, hf = scratch[:, 0, :], scratch[:, 1, :]
        h_hi = sb("h_hi", [P, 2, T], F32R)
        h_lo = sb("h_lo", [P, 2, T], F32R)
        hl_hi = sb("hl_hi", [P, 2, T], F32R)
        hl_lo = sb("hl_lo", [P, 2, T], F32R)
        sx_hi = sb("sx_hi", [P, 2, T], F32R)
        sx_lo = sb("sx_lo", [P, 2, T], F32R)
        SP_HI = [flat(t) for t in (h_hi, hl_hi, sx_hi)]
        SP_LO = [flat(t) for t in (h_lo, hl_lo, sx_lo)]
        lnp = sb("lnp", [P, 2, D])
        mixg = sb("mixg", [P, KC])
        band = sb("band", [P, HEADS, T])
        qT = sb("qT", [P, 8, T])
        kpad = sb("kpad", [P, 16, T])
        v = sb("v", [P, 2, D])
        ez = sb("ez", [P, 2, 512])
        soft_t = sb("soft_t", [P, HEADS, T + P])
        stick_t = sb("stick_t", [P, HEADS, T + P])
        table = sb("table", [P, 5, P])
        ident, neg_tri, neg_one, flip, head_mean = (table[:, i, :] for i in range(5))
        neg_r = sb("neg_r", [P, 2, P], F32R)
        eps = sb("eps", [P, 2])
        sums = sb("sums", [P, 2, 4])
        lt = sb("lt", [P, 2, 5])
        mx = sb("mx", [P, 16])
        nmx = sb("nmx", [P, 16])
        se = sb("se", [P, 16])
        rinv = sb("rinv", [P, 16])

        bank = [ctx.enter_context(nc.psum_tensor(f"bank{i}", [P, 512], F32)) for i in range(8)]
        Y = [[bank[4], bank[5]], [bank[6], bank[7]]]
        Z = [bank[2], bank[3]]
        refine = [sg, hf]
        SS = [bank[2], bank[3]]
        O = [[bank[4], bank[5]], [bank[0], bank[1]]]

        raw_ready = [sem(f"raw_ready{s}") for s in range(3)]
        half_ready = sem("half_ready")
        hi_ready = sem("hi_ready")
        lo_ready = sem("lo_ready")
        unit_used = sem("unit_used")
        x_loaded = sem("x_loaded")
        xT_loaded = [sem(f"xT_loaded{half}") for half in range(2)]
        first_hi = sem("first_hi")
        first_lo = sem("first_lo")
        consts = sem("consts")
        kzero = sem("kzero")
        pool_steps = sem("pool_steps")
        xn_done = sem("xn_done")
        xt_done = sem("xt_done")
        xhi_done = sem("xhi_done")
        xlo_done = sem("xlo_done")
        y_done = sem("y_done")
        rstd_done = sem("rstd_done")
        silu_done = sem("silu_done")
        hf_done = sem("hf_done")
        hhi_done = sem("hhi_done")
        hlo_done = sem("hlo_done")
        lnp_ready = sem("lnp_ready")
        att_par = sem("att_par")
        band_ready = sem("band_ready")
        band_mm = sem("band_mm")
        band_turned = sem("band_turned")
        ln_step = sem("ln_step")
        var_done = sem("var_done")
        lnv_done = sem("lnv_done")
        unit_evac = sem("unit_evac")
        z_done = sem("z_done")
        az_done = sem("az_done")
        ez_done = sem("ez_done")
        lz_done = sem("lz_done")
        sp_done = sem("sp_done")
        spm_done = sem("spm_done")
        sp_hi_done = sem("sp_hi_done")
        sp_lo_done = sem("sp_lo_done")
        neg_ready = sem("neg_ready")
        c_done = sem("c_done")
        w_done = sem("w_done")
        wm_done = sem("wm_done")
        t_done = sem("t_done")
        sa_done = sem("sa_done")
        mx_done = sem("mx_done")
        nm_done = sem("nm_done")
        p_done = sem("p_done")
        x_done = sem("x_done")
        pt_done = sem("pt_done")
        rinv_done = sem("rinv_done")
        pn_done = sem("pn_done")
        o_done = sem("o_done")
        sq_done = sem("sq_done")
        ss_done = sem("ss_done")
        lnr_done = sem("lnr_done")
        rr_done = sem("rr_done")
        rsq_done = sem("rsq_done")
        newton = sem("newton")
        gain_ready = sem("gain_ready")
        mix_done = sem("mix_done")
        mhi_done = sem("mhi_done")
        mlo_done = sem("mlo_done")
        stored = sem("stored")

        def used(l, rel):
            return l * UNITS + (rel + 4)

        def split(l, rel):
            return l * UNITS + (rel + 4)

        def by_head(tile, heads):
            return tile[:, :].rearrange("p (h s) -> p h s", h=len(heads))

        def it(l, f, j):
            return l * (2 * FP) + (f * FP) + j

        def phase(l, p):
            return l * 3 + p

        HALVES = [slice(0, UW // 2), slice(UW // 2, UW)]

        def loaded(l, slot, filled):
            return l * (16 * PER_LAYER[slot]) + 16 * (filled + 1)

        block = ctx.enter_context(nc.Block())

        @block.sync
        def _(sp):
            def load(slot, n, back=3, source=None):
                sp.wait_ge(lo_ready, n + (4 - back))
                n = n if source is None else source
                if slot == 0:
                    for c, ready in zip(HALVES, (half_ready, raw_ready[0])):
                        sp.dma_start(raw[:, 0, c], stream[n][:, c]).then_inc(ready, 16)
                else:
                    sp.dma_start(raw[:, slot, :], stream[n]).then_inc(raw_ready[slot], 16)

            sp.dma_start(qT[:, 0:4, :], xT_in[:, 0:4, :]).then_inc(xT_loaded[0], 16)
            sp.sem_inc(lo_ready, 3)
            with sp.Fori(0, DEPTH) as l:
                with sp.Fori(0, (FFN_UNITS + WIN_UNITS) // 3) as i:
                    for s in range(3):
                        load(s, l * UNITS + i * 3 + s)
                for a in range(WOUT_UNITS):
                    rel = ATT0 + WIN_UNITS + a
                    load(SLOT[rel], l * UNITS + rel, back=2 if a == 0 else 3)
                for s in range(3):
                    load(s, l * UNITS + FFN_BASE[1] + s, back=2 if s == 1 else 3)
                with sp.Fori(1, FFN_UNITS // 3) as i:
                    for s in range(3):
                        load(s, l * UNITS + FFN_BASE[1] + i * 3 + s)
            load(0, DEPTH * UNITS, source=DEPTH * UNITS - 1)
            for tb in range(2):
                for half in range(2):
                    cols = slice(512 * half, 512 * half + 512)
                    sp.wait_ge(xn_done, 4 * (3 * DEPTH) + (2 * tb + half + 1))
                    sp.dma_start(out[tb * P:(tb + 1) * P, cols], xn[:, tb, cols]).then_inc(stored, 16)
            sp.wait_ge(stored, 64)

        @block.gpsimd
        def _(pool):
            nc.gpsimd.memset(ident, 0.0).then_inc(consts, 1)
            nc.gpsimd.memset(neg_tri, -1.0).then_inc(consts, 1)
            nc.gpsimd.memset(neg_one, -1.0).then_inc(consts, 1)
            nc.gpsimd.memset(flip, 0.0).then_inc(consts, 1)
            nc.gpsimd.memset(eps[:, 0:1], LN_EPS).then_inc(consts, 1)
            nc.gpsimd.memset(eps[:, 1:2], RMS_EPS).then_inc(consts, 1)
            nc.gpsimd.memset(head_mean, 0.0).then_inc(consts, 1)
            pool.wait_ge(consts, 7)
            nc.gpsimd.affine_select(out=ident, in_=ident, compare_op=ALU.not_equal, fill=1.0,
                                    base=0, pattern=[[-1, P]], channel_multiplier=1).then_inc(consts, 1)
            nc.gpsimd.affine_select(out=neg_tri, in_=neg_tri, compare_op=ALU.is_ge, fill=0.0,
                                    base=0, pattern=[[-1, P]], channel_multiplier=1).then_inc(consts, 1)
            nc.gpsimd.affine_select(out=flip, in_=flip, compare_op=ALU.not_equal, fill=1.0,
                                    base=1 - P, pattern=[[1, P]], channel_multiplier=1).then_inc(consts, 1)
            pool.wait_ge(consts, 10)
            nc.gpsimd.memset(head_mean[0:HD, 0:HD], 1.0 / HD).then_inc(consts, 1)
            pool.wait_ge(consts, 11)
            nc.gpsimd.memset(head_mean[HD:P, HD:P], 1.0 / HD).then_inc(consts, 1)
            pool.wait_ge(consts, 12)
            nc.gpsimd.memset(kpad[:, :, :], 0.0).then_inc(kzero, 1)

            def load_lnp(l, p):
                pool.wait_ge(xn_done, phase(l, p) * 4 + 4)
                pool.dma_start(lnp[:, :, :], ln_gb[phase(l, p)].partition_broadcast(P)).then_inc(lnp_ready, 16)

            def wait_alone(semaphore, value):
                pool.wait_ge(semaphore, value)
                pool.sem_inc(pool_steps, 1)

            def causal(tiles, b, done):
                view = sb_view(tiles, b)[:, :, 0:P]
                nc.gpsimd.affine_select(out=view, in_=view, compare_op=ALU.is_gt, fill=0.0, base=0,
                                        pattern=[[0, len(SB_BANKS[b][1])], [1, P]],
                                        channel_multiplier=-1).then_inc(done, 1)

            pool.wait_ge(raw_ready[2], 16)
            pool.dma_start(xn[:, :, :], x_in.rearrange("(b p) d -> p b d", p=P)).then_inc(x_loaded, 16)
            pool.wait_ge(x_loaded, 16)
            pool.sem_inc(xn_done, 4)
            with pool.Fori(0, DEPTH) as l:
                load_lnp(l, 0)
                pool.dma_start(mixg[:, :], mix_g[l]).then_inc(att_par, 16)
                src = bass.AP(rel_band.tensor, l * (HEADS * BAND), [[1, P], [BAND, HEADS], [1, T]])
                pool.dma_start(flat(soft_t)[:, 0:HEADS * T].rearrange("p (h s) -> p h s", h=HEADS),
                               src).then_inc(att_par, 16)
                wait_alone(att_par, (l + 1) * 32)
                nc.gpsimd.tensor_scalar(mixg[:, :], mixg[:, :], -0.5, None, ALU.mult).then_inc(gain_ready, 1)
                wait_alone(band_turned, (l + 1) * 4)
                nc.gpsimd.memset(band[0:64, :, 192:256], NEG).then_inc(band_ready, 1)
                load_lnp(l, 1)
                for b in range(7):
                    if b < 6:
                        wait_alone(sp_done, l * 6 + (b + 1))
                        causal(stick_t, b, spm_done)
                    if b > 0:
                        wait_alone(w_done, l * 6 + b)
                        causal(stick_t, b - 1, wm_done)
                load_lnp(l, 2)

        @block.scalar
        def _(act):
            nc.scalar.preload_act_table(ACT.Silu)
            act.sem_inc(unit_used, 3)
            act.dma_start(qT[:, 4:8, :], xT_in[:, 4:8, :]).then_inc(xT_loaded[1], 16)

            def split_hi(l, rel, slot, filled):
                act.wait_ge(raw_ready[slot], loaded(l, slot, filled))
                if slot == 0:
                    act.wait_ge(half_ready, loaded(l, slot, filled))
                act.wait_ge(unit_used, used(l, rel - 3))
                nc.scalar.activation(w_hi[:, slot, :], raw[:, slot, :], ACT.Copy).then_inc(hi_ready, 1)

            def split_first_hi(l, rel, filled):
                act.wait_ge(unit_used, used(l, rel - 3))
                for c, ready, done in zip(HALVES, (half_ready, raw_ready[0]), (first_hi, hi_ready)):
                    act.wait_ge(ready, loaded(l, 0, filled))
                    nc.scalar.activation(w_hi[:, 0, c], raw[:, 0, c], ACT.Copy).then_inc(done, 1)

            def split_hi_at(l, rel):
                if rel == ATT0 + WIN_UNITS:
                    act.wait_ge(unit_used, used(l, rel - 2))
                split_hi(l, rel, SLOT[rel], FILLED[rel])

            def x_hi(count, g):
                tb, half = divmod(g, 2)
                act.wait_ge(xt_done, (count - 1) * 4 + (g + 1))
                nc.scalar.activation(xT_hi[:, 4 * half:4 * half + 4, tb * P:(tb + 1) * P],
                                     bank[g][:, :].rearrange("p (c t) -> p c t", c=4),
                                     ACT.Copy).then_inc(xhi_done, 1)

            def rstd(l, p, tb):
                n = phase(l, p) * 2 + tb
                act.wait_ge(ln_step, n * LN_STEPS + LN_MEAN)
                nc.scalar.activation(flat(scratch), xn[:, tb, :], ACT.Square, bias=sums[:, tb, 2:3],
                                     accum_out=sums[:, tb, 3:4]).then_inc(var_done, 1)
                act.wait_ge(var_done, n + 1)
                nc.scalar.activation(lt[:, tb, 0:1], sums[:, tb, 3:4], ACT.Ln, scale=1.0 / D,
                                     bias=eps[:, 0:1]).then_inc(lnv_done, 1)
                act.wait_ge(lnv_done, n + 1)
                nc.scalar.activation(lt[:, tb, 1:2], lt[:, tb, 0:1], ACT.Exp, scale=-0.5).then_inc(rstd_done, 1)

            def after_ln(l, p):
                count = phase(l, p + 1)
                rstd(l, p, 0)
                x_hi(count, 0)
                rstd(l, p, 1)
                x_hi(count, 1)
                if p == 0:
                    band_out(l, 0)
                    band_out(l, 1)
                else:
                    nc.scalar.preload_act_table(ACT.Silu)
                x_hi(count, 2)
                x_hi(count, 3)
                if p == 0:
                    band_out(l, 2)
                    band_out(l, 3)

            def ffn(l, f):
                base = FFN_BASE[f]
                first = FILLED[base:base + 3]

                def silu(j, rel):
                    act.wait_ge(unit_used, used(l, base + rel))
                    nc.scalar.activation(sg, bank[0][:, :], ACT.Silu).then_inc(silu_done, 1)

                if f == 1:
                    act.wait_ge(unit_used, used(l, base - 1))
                split_hi(l, base + 1, 1, first[1])
                split_hi(l, base + 2, 2, first[2])
                silu(0, 0)
                split_hi(l, base + 3, 0, first[0] + 1)

                def h_high(j, hi):
                    act.wait_ge(hf_done, it(l, f, j) + 1)
                    nc.scalar.activation(hi[:, :, :], hf.rearrange("p (c t) -> p c t", c=2),
                                         ACT.Copy).then_inc(hhi_done, 1)

                def step(j):
                    act.wait_ge(unit_used, used(l, base + 3 * j + 1))
                    h_high(j, h_hi)
                    split_hi(l, base + 3 * j + 4, 1, first[1] + 1 + j)
                    split_hi(l, base + 3 * j + 5, 2, first[2] + 1 + j)
                    silu(j + 1, 3 * j + 2)

                with act.Fori(0, FP - 2) as j:
                    step(j)
                    split_hi(l, base + 3 * j + 6, 0, first[0] + 2 + j)
                step(FP - 2)
                h_high(FP - 1, hl_hi)
                split_first_hi(l, base + FFN_UNITS, first[0] + FP)
                nc.scalar.preload_act_table_set("natural_log_exp_and_others")

            def band_out(l, i):
                act.wait_ge(band_mm, l * 4 + (i + 1))
                nc.scalar.activation(band[:, 2 * i:2 * i + 2, :],
                                     bank[4 + i][:, :].rearrange("p (h s) -> p h s", h=2),
                                     ACT.Copy).then_inc(band_turned, 1)

            def evacuate(l, a):
                kind, part, half = W_IN[a]
                two = bank[a % 2][:, :].rearrange("p (c t) -> p c t", c=2)
                act.wait_ge(unit_used, used(l, ATT0 + a))
                if kind == "q":
                    nc.scalar.activation(qT[:, 4 * part + 2 * half:4 * part + 2 * half + 2, :], two,
                                         ACT.Copy, scale=QSCALE).then_inc(unit_evac, 1)
                elif kind == "k":
                    h0 = 8 * part + 4 * half
                    nc.scalar.activation(kpad[0:64, h0:h0 + 4:2, :], two[0:64], ACT.Copy)
                    nc.scalar.activation(kpad[64:128, h0 + 1:h0 + 4:2, :], two[64:128],
                                         ACT.Copy).then_inc(unit_evac, 1)
                else:
                    c0 = 512 * part + 256 * half
                    nc.scalar.activation(v[:, :, c0:c0 + 256], two, ACT.Copy).then_inc(unit_evac, 1)

            def log_keep(l, b):
                e = ez[:, b % 2, :]
                act.wait_ge(z_done, l * 6 + (b + 1))
                if b >= 2:
                    act.wait_ge(sp_done, l * 6 + (b - 1))
                nc.scalar.activation(e, Z[b % 2][:, :], ACT.Abs).then_inc(az_done, 1)
                act.wait_ge(az_done, l * 6 + (b + 1))
                nc.scalar.activation(e, e, ACT.Exp, scale=-1.0).then_inc(ez_done, 1)
                act.wait_ge(ez_done, l * 6 + (b + 1))
                nc.scalar.activation(e, e, ACT.Ln, bias=1.0).then_inc(lz_done, 1)

            def softplus_hi(l, b):
                act.wait_ge(spm_done, l * 6 + (b + 1))
                if b >= 3:
                    act.wait_ge(c_done, l * 6 + (3, 2, 3)[b - 3])
                nc.scalar.activation(by_head(SP_HI[b % 3], SB_BANKS[b][1]), sb_view(stick_t, b),
                                     ACT.Copy).then_inc(sp_hi_done, 1)

            def weights(l, b):
                act.wait_ge(c_done, l * 6 + (b + 1))
                nc.scalar.activation(sb_view(stick_t, b), by_head(Z[b % 2], SB_BANKS[b][1]),
                                     ACT.Exp).then_inc(w_done, 1)

            def softmax_exp(l, b):
                qb, heads = CA_BANKS[b]
                act.wait_ge(nm_done, l * 6 + (b + 1))
                for i, h in enumerate(heads):
                    c = 8 * qb + h
                    s = ca_view(soft_t, b)[:, i, :]
                    last = nc.scalar.activation(s, s,
                                                ACT.Exp, bias=nmx[:, c:c + 1], accum_out=se[:, c:c + 1])
                last.then_inc(p_done, 1)

            def square(l, part, i):
                g = l * 4 + (2 * part + i)
                act.wait_ge(o_done, g + 1)
                if part == 1:
                    act.wait_ge(mix_done, g - 1)
                nc.scalar.activation(ez[:, i, :], O[part][i][:, :], ACT.Square).then_inc(sq_done, 1)

            def head_rstd(l, part, i):
                g = l * 4 + (2 * part + i)
                act.wait_ge(ss_done, g + 1)
                nc.scalar.activation(ez[:, i, :], SS[i][:, :], ACT.Ln, bias=eps[:, 1:2]).then_inc(lnr_done, 1)
                act.wait_ge(lnr_done, g + 1)
                nc.scalar.activation(ez[:, i, :], ez[:, i, :], ACT.Exp, scale=-0.5).then_inc(rr_done, 1)
                act.wait_ge(rr_done, g + 1)
                nc.scalar.activation(refine[i], ez[:, i, :], ACT.Square).then_inc(rsq_done, 1)

            def turned(l, b):
                act.wait_ge(x_done, l * 6 + (b + 1))
                nc.scalar.activation(ca_view(soft_t, b), by_head(bank[7], CA_BANKS[b][1]),
                                     ACT.Copy).then_inc(pt_done, 1)

            def mixed_hi(l, part, i):
                act.wait_ge(unit_used, used(l, ATT0 + WIN_UNITS - 1))
                act.wait_ge(mix_done, l * 4 + (2 * part + i + 1))
                c = slice(4 * part + 2 * i, 4 * part + 2 * i + 2)
                nc.scalar.activation(xT_hi[:, c, :], qT[:, c, :], ACT.Copy).then_inc(mhi_done, 1)

            def attention(l):
                act.wait_ge(kzero, 1)
                split_hi_at(l, ATT0 + 1)
                split_hi_at(l, ATT0 + 2)
                for a in range(3):
                    evacuate(l, a)
                    split_hi_at(l, ATT0 + a + 3)
                evacuate(l, 3)
                split_hi_at(l, ATT0 + 6)
                log_keep(l, 0)
                softplus_hi(l, 0)
                for b in range(4):
                    log_keep(l, b + 1)
                    evacuate(l, 4 + b)
                    if b == 0:
                        weights(l, b)
                        softplus_hi(l, b + 1)
                    else:
                        softplus_hi(l, b + 1)
                        weights(l, b)
                    split_hi_at(l, ATT0 + 7 + b)
                softmax_exp(l, 0)
                log_keep(l, 5)
                evacuate(l, 8)
                softplus_hi(l, 5)
                softmax_exp(l, 1)
                weights(l, 4)
                split_hi_at(l, ATT0 + 11)
                evacuate(l, 9)
                weights(l, 5)
                softmax_exp(l, 2)
                softmax_exp(l, 3)
                square(l, 0, 0)
                square(l, 0, 1)
                softmax_exp(l, 4)
                evacuate(l, 10)
                head_rstd(l, 0, 0)
                head_rstd(l, 0, 1)
                softmax_exp(l, 5)
                split_hi_at(l, ATT0 + 12)
                turned(l, 4)
                evacuate(l, 11)
                turned(l, 5)
                mixed_hi(l, 0, 0)
                split_hi_at(l, ATT0 + 13)
                square(l, 1, 0)
                mixed_hi(l, 0, 1)
                square(l, 1, 1)
                split_hi_at(l, ATT0 + 14)
                head_rstd(l, 1, 0)
                head_rstd(l, 1, 1)
                split_hi_at(l, ATT0 + 15)
                mixed_hi(l, 1, 0)
                mixed_hi(l, 1, 1)
                split_first_hi(l, FFN_BASE[1], FILLED[FFN_BASE[1]])

            for half, c in enumerate(HALVES):
                part = slice(4 * half, 4 * half + 4)
                act.wait_ge(xT_loaded[half], 16)
                nc.scalar.activation(xT_hi[:, part, :], qT[:, part, :], ACT.Copy).then_inc(xhi_done, (3, 1)[half])
                act.wait_ge((half_ready, raw_ready[0])[half], 16)
                nc.scalar.activation(w_hi[:, 0, c], raw[:, 0, c], ACT.Copy).then_inc((first_hi, hi_ready)[half], 1)
            act.wait_ge(consts, 12)
            nc.scalar.activation(neg_r[:, :, :], table[:, 1:3, :], ACT.Copy).then_inc(neg_ready, 1)
            with act.Fori(0, DEPTH) as l:
                ffn(l, 0)
                after_ln(l, 0)
                attention(l)
                after_ln(l, 1)
                ffn(l, 1)
                after_ln(l, 2)

        @block.vector
        def _(dve):
            def split_lo(l, rel, slot):
                dve.wait_ge(hi_ready, l * UNITS + (rel + 1))
                nc.vector.tensor_tensor(w_lo[:, slot, :], raw[:, slot, :], w_hi[:, slot, :].bitcast(F32),
                                        ALU.subtract).then_inc(lo_ready, 1)

            def split_half_lo(half):
                c = HALVES[half]
                nc.vector.tensor_tensor(w_lo[:, 0, c], raw[:, 0, c], w_hi[:, 0, c].bitcast(F32),
                                        ALU.subtract).then_inc((first_lo, lo_ready)[half], 1)

            def split_first_lo(l, p, rel):
                dve.wait_ge(first_hi, phase(l, p) + 1)
                split_half_lo(0)
                dve.wait_ge(hi_ready, l * UNITS + (rel + 1))
                split_half_lo(1)

            def x_lo(count, groups):
                for g in groups:
                    tb, half = divmod(g, 2)
                    dve.wait_ge(xhi_done, count * 4 + (g + 1))
                    part = slice(4 * half, 4 * half + 4), slice(tb * P, (tb + 1) * P)
                    nc.vector.tensor_tensor(xT_lo[:, part[0], part[1]],
                                            bank[g][:, :].rearrange("p (c t) -> p c t", c=4),
                                            xT_hi[:, part[0], part[1]].bitcast(F32),
                                            ALU.subtract).then_inc(xlo_done, 1)

            def layer_norm(l, p):
                dve.wait_ge(xn_done, phase(l, p) * 4 + 4)
                dve.wait_ge(lnp_ready, phase(l, p) * 16 + 16)
                for tb in range(2):
                    n = phase(l, p) * 2 + tb
                    k = [0]

                    def done(ins):
                        k[0] += 1
                        ins.then_inc(ln_step, 1)

                    def after(count):
                        dve.wait_ge(ln_step, n * LN_STEPS + count)

                    halves = [slice(512 * half, 512 * half + 512) for half in range(2)]
                    for half, cols in enumerate(halves):
                        dve.wait_ge(y_done, n * 2 + (half + 1))
                        done(nc.vector.scalar_tensor_tensor(out=xn[:, tb, cols], in0=xn[:, tb, cols],
                                                            scalar=ALPHA, in1=Y[tb][half][:, :],
                                                            op0=ALU.mult, op1=ALU.add,
                                                            accum_out=sums[:, tb, half:half + 1]))
                    after(k[0])
                    minus_mean = sums[:, tb, 2:3]
                    done(nc.vector.tensor_scalar(minus_mean, sums[:, tb, 0:1], sums[:, tb, 1:2], -1.0 / D,
                                                 ALU.add, ALU.mult))
                    assert k[0] == LN_MEAN
                    after(k[0])
                    for cols in halves:
                        done(nc.vector.scalar_tensor_tensor(out=centred[:, tb, cols], in0=xn[:, tb, cols],
                                                            scalar=minus_mean, in1=lnp[:, 0, cols],
                                                            op0=ALU.add, op1=ALU.mult))
                    if tb == 1:
                        x_lo(phase(l, p + 1), (0,))
                    dve.wait_ge(var_done, n + 1)
                    done(nc.vector.tensor_scalar(lt[:, tb, 2:3], sums[:, tb, 3:4], -0.5 / D, -0.5 * LN_EPS,
                                                 ALU.mult, ALU.add))
                    after(k[0])
                    dve.wait_ge(rstd_done, n + 1)
                    y = lt[:, tb, 1:2]
                    done(nc.vector.tensor_scalar(lt[:, tb, 3:4], y, y, lt[:, tb, 2:3], ALU.mult, ALU.mult))
                    after(k[0])
                    done(nc.vector.tensor_scalar(lt[:, tb, 4:5], lt[:, tb, 3:4], 1.5, y, ALU.add, ALU.mult))
                    assert k[0] == LN_STEPS
                    after(k[0])
                    for cols in halves:
                        nc.vector.scalar_tensor_tensor(out=xn[:, tb, cols], in0=centred[:, tb, cols],
                                                       scalar=lt[:, tb, 4:5], in1=lnp[:, 1, cols],
                                                       op0=ALU.mult, op1=ALU.add).then_inc(xn_done, 1)
                x_lo(phase(l, p + 1), (1, 2, 3))

            def ffn(l, f):
                base = FFN_BASE[f]

                def gated(step, rel, first=False):
                    if not first:
                        dve.wait_ge(hlo_done, step)
                    dve.wait_ge(silu_done, step + 1)
                    dve.wait_ge(unit_used, used(l, base + rel))
                    nc.vector.scalar_tensor_tensor(out=hf, in0=sg, scalar=0.5, in1=bank[1][:, :], op0=ALU.mult,
                                                   op1=ALU.mult).then_inc(hf_done, 1)

                def h_low(step, hi, lo):
                    dve.wait_ge(hhi_done, step + 1)
                    nc.vector.tensor_tensor(lo[:, :, :], hf.rearrange("p (c t) -> p c t", c=2),
                                            hi[:, :, :].bitcast(F32), ALU.subtract).then_inc(hlo_done, 1)

                split_lo(l, base + 1, 1)
                split_lo(l, base + 2, 2)
                gated(it(l, f, 0), 1, first=True)
                split_lo(l, base + 3, 0)

                def step(j):
                    h_low(it(l, f, j), h_hi, h_lo)
                    split_lo(l, base + 3 * j + 4, 1)
                    split_lo(l, base + 3 * j + 5, 2)
                    gated(it(l, f, j) + 1, 3 * j + 3)

                with dve.Fori(0, FP - 2) as j:
                    step(j)
                    split_lo(l, base + 3 * j + 6, 0)
                step(FP - 2)
                h_low(it(l, f, FP - 1), hl_hi, hl_lo)
                split_first_lo(l, 2 * f + 1, base + FFN_UNITS)

            def split_lo_at(l, rel):
                split_lo(l, rel, SLOT[rel])

            def softplus(l, b):
                dve.wait_ge(lz_done, l * 6 + (b + 1))
                nc.vector.scalar_tensor_tensor(out=sb_view(stick_t, b), in0=by_head(Z[b % 2], SB_BANKS[b][1]),
                                               scalar=0.0, in1=by_head(ez[:, b % 2, :], SB_BANKS[b][1]),
                                               op0=ALU.max, op1=ALU.add).then_inc(sp_done, 1)

            def softplus_lo(l, b):
                heads = SB_BANKS[b][1]
                dve.wait_ge(sp_hi_done, l * 6 + (b + 1))
                nc.vector.tensor_tensor(by_head(SP_LO[b % 3], heads), sb_view(stick_t, b),
                                        by_head(SP_HI[b % 3], heads).bitcast(F32),
                                        ALU.subtract).then_inc(sp_lo_done, 1)

            def scores(l, b):
                qb, heads = CA_BANKS[b]
                n, m = len(heads), 512 // len(heads)
                s = ca_view(soft_t, b)
                c = slice(8 * qb + heads[0], 8 * qb + heads[0] + n)
                dve.wait_ge(t_done, l * 6 + (b + 1))
                nc.vector.tensor_tensor(s, by_head(bank[6], heads),
                                        band[:, heads[0]:heads[0] + n, T - m:T], ALU.add).then_inc(sa_done, 1)
                dve.wait_ge(sa_done, l * 6 + (b + 1))
                nc.vector.tensor_reduce(mx[:, c], s, AX_X, ALU.max).then_inc(mx_done, 1)
                dve.wait_ge(mx_done, l * 6 + (b + 1))
                nc.vector.tensor_scalar(nmx[:, c], mx[:, c], -1.0, None, ALU.mult).then_inc(nm_done, 1)

            def normalise(l, b):
                qb, heads = CA_BANKS[b]
                c = slice(8 * qb + heads[0], 8 * qb + heads[-1] + 1)
                s = ca_view(soft_t, b)
                dve.wait_ge(p_done, l * 6 + (b + 1))
                nc.vector.reciprocal(rinv[:, c], se[:, c]).then_inc(rinv_done, 1)
                dve.wait_ge(rinv_done, l * 6 + (b + 1))
                r = rinv[:, c].unsqueeze(2).to_broadcast([P, len(heads), 512 // len(heads)])
                nc.vector.tensor_tensor(s, s, r, ALU.mult).then_inc(pn_done, 1)

            def turned(l, b):
                dve.wait_ge(x_done, l * 6 + (b + 1))
                nc.vector.tensor_copy(ca_view(soft_t, b), by_head(bank[7], CA_BANKS[b][1])).then_inc(pt_done, 1)

            def mix(l, part, i):
                g = l * 4 + (2 * part + i)
                y2, y = refine[i], ez[:, i, :]
                if part == 0 and i == 0:
                    dve.wait_ge(gain_ready, l + 1)
                dve.wait_ge(rsq_done, g + 1)
                nc.vector.scalar_tensor_tensor(out=y2, in0=SS[i][:, :], scalar=RMS_EPS, in1=y2,
                                               op0=ALU.add, op1=ALU.mult).then_inc(newton, 1)
                dve.wait_ge(newton, 2 * g + 1)
                nc.vector.scalar_tensor_tensor(out=y, in0=y2, scalar=-3.0, in1=y,
                                               op0=ALU.add, op1=ALU.mult).then_inc(newton, 1)
                dve.wait_ge(newton, 2 * g + 2)
                for k in range(2):
                    c = 4 * part + 2 * i + k
                    last = nc.vector.scalar_tensor_tensor(
                        out=qT[:, c, :], in0=O[part][i][:, k * T:(k + 1) * T], scalar=mixg[:, c:c + 1],
                        in1=ez[:, i, k * T:(k + 1) * T], op0=ALU.mult, op1=ALU.mult)
                last.then_inc(mix_done, 1)

            def mixed_lo(l, part, i):
                dve.wait_ge(mhi_done, l * 4 + (2 * part + i + 1))
                c = slice(4 * part + 2 * i, 4 * part + 2 * i + 2)
                nc.vector.tensor_tensor(xT_lo[:, c, :], qT[:, c, :], xT_hi[:, c, :].bitcast(F32),
                                        ALU.subtract).then_inc(mlo_done, 1)

            def attention(l):
                for rel in range(1, 7):
                    split_lo_at(l, ATT0 + rel)
                softplus(l, 0)
                softplus_lo(l, 0)
                for b in range(4):
                    softplus(l, b + 1)
                    softplus_lo(l, b + 1)
                    if b == 3:
                        dve.wait_ge(band_ready, l + 1)
                        scores(l, 0)
                    split_lo_at(l, ATT0 + 7 + b)
                normalise(l, 0)
                scores(l, 1)
                softplus(l, 5)
                softplus_lo(l, 5)
                normalise(l, 1)
                turned(l, 0)
                scores(l, 2)
                split_lo_at(l, ATT0 + 11)
                turned(l, 1)
                scores(l, 3)
                normalise(l, 2)
                normalise(l, 3)
                turned(l, 2)
                scores(l, 4)
                normalise(l, 4)
                turned(l, 3)
                scores(l, 5)
                mix(l, 0, 0)
                normalise(l, 5)
                split_lo_at(l, ATT0 + 12)
                mixed_lo(l, 0, 0)
                mix(l, 0, 1)
                mixed_lo(l, 0, 1)
                split_lo_at(l, ATT0 + 13)
                split_lo_at(l, ATT0 + 14)
                mix(l, 1, 0)
                mix(l, 1, 1)
                mixed_lo(l, 1, 0)
                mixed_lo(l, 1, 1)
                split_lo_at(l, ATT0 + 15)
                split_first_lo(l, 2, FFN_BASE[1])

            for half in range(2):
                part = slice(4 * half, 4 * half + 4)
                dve.wait_ge(xhi_done, (3, 4)[half])
                nc.vector.tensor_tensor(xT_lo[:, part, :], qT[:, part, :], xT_hi[:, part, :].bitcast(F32),
                                        ALU.subtract).then_inc(xlo_done, (3, 1)[half])
                dve.wait_ge((first_hi, hi_ready)[half], 1)
                split_half_lo(half)
            with dve.Fori(0, DEPTH) as l:
                ffn(l, 0)
                layer_norm(l, 0)
                attention(l)
                layer_norm(l, 1)
                ffn(l, 1)
                layer_norm(l, 2)

        @block.tensor
        def _(pe):
            def three(o, w, x, start, stop):
                nc.tensor.matmul(o, w[0], x[0], start=start, stop=False)
                nc.tensor.matmul(o, w[0], x[1], start=False, stop=False)
                return nc.tensor.matmul(o, w[1], x[0], start=False, stop=stop)

            def columns(l, rel, slot, out_bank, halves=(0, 1)):
                pe.wait_ge(lo_ready, split(l, rel))
                for c in halves:
                    for kc in range(KC):
                        w = slice(kc * 256 + c * P, kc * 256 + (c + 1) * P)
                        last = three(out_bank[:, c * T:(c + 1) * T], (w_hi[:, slot, w], w_lo[:, slot, w]),
                                     (xT_hi[:, kc, :], xT_lo[:, kc, :]), kc == 0, kc == KC - 1)
                if halves[-1] == 1:
                    last.then_inc(unit_used, 1)

            def rows(l, rel, slot, out_bank, halves=(0, 1)):
                pe.wait_ge(lo_ready, split(l, rel))
                for tb in halves:
                    for kc in range(KC):
                        w = slice(kc * 256, (kc + 1) * 256)
                        t = slice(tb * P, (tb + 1) * P)
                        last = three(out_bank[:, tb * 256:(tb + 1) * 256], (xT_hi[:, kc, t], xT_lo[:, kc, t]),
                                     (w_hi[:, slot, w], w_lo[:, slot, w]), kc == 0, kc == KC - 1)
                if halves[-1] == 1:
                    last.then_inc(unit_used, 1)

            def down(slot, hi, lo, c0, tbs, start=False, stop=False, halves=(0, 1)):
                for tb in tbs:
                    for half in halves:
                        for c in range(2):
                            w = slice(c * D + half * 512, c * D + half * 512 + 512)
                            t = slice(tb * P, (tb + 1) * P)
                            last = three(Y[tb][half][:, :], (hi[:, c0 + c, t], lo[:, c0 + c, t]),
                                         (w_hi[:, slot, w], w_lo[:, slot, w]),
                                         start and c == 0, stop and c == 1)
                return last

            def turn_x(tb, count):
                for half in range(2):
                    pe.wait_ge(xn_done, count * 4 + (2 * tb + half + 1))
                    for q in range(4):
                        c = (4 * half + q) * P
                        last = nc.tensor.transpose(bank[2 * tb + half][:, q * P:(q + 1) * P],
                                                   xn[:, tb, c:c + P], ident)
                    last.then_inc(xt_done, 1)

            def turn_band(l, i):
                if i == 0:
                    pe.wait_ge(att_par, (l + 1) * 32)
                if i == 2:
                    pe.wait_ge(ln_step, (phase(l, 0) * 2 + 1) * LN_STEPS + LN_MEAN)
                nc.tensor.matmul(bank[4 + i][:, :], flip, flat(soft_t)[:, i * 512:(i + 1) * 512], start=True,
                                 stop=True).then_inc(band_mm, 1)

            def keep_warm(count):
                for i in range(count):
                    nc.tensor.matmul(bank[3][:, :], ident, flat(table)[:, 0:512],
                                     start=True, stop=True)

            def first_columns(l, rel, count):
                def products(kh, w, x):
                    for c in range(2):
                        for kc in range(4 * kh, 4 * kh + 4):
                            last = plain(bank[0][:, c * T:(c + 1) * T],
                                         w[:, 0, kc * 256 + c * P:kc * 256 + (c + 1) * P], x[:, kc, :],
                                         start=w is w_hi and x is xT_hi and kc == 0 and c == 0,
                                         stop=x is xT_lo and kc == KC - 1)
                    return last

                pe.wait_ge(xlo_done, count * 4 + 1)
                for kh in range(2):
                    pe.wait_ge(xhi_done, count * 4 + (3 + kh))
                    if kh == 0:
                        pe.wait_ge(first_hi, count + 1)
                    else:
                        pe.wait_ge(hi_ready, l * UNITS + (rel + 1))
                    products(kh, w_hi, xT_hi)
                    if kh == 0:
                        pe.wait_ge(first_lo, count + 1)
                    else:
                        pe.wait_ge(lo_ready, split(l, rel))
                    products(kh, w_lo, xT_hi)
                for kh in range(2):
                    pe.wait_ge(xlo_done, count * 4 + (3 + kh))
                    last = products(kh, w_hi, xT_lo)
                last.then_inc(unit_used, 1)

            def plain(o, w, x, start=False, stop=False):
                return nc.tensor.matmul(o, w, x, start=start, stop=stop, skip_group_check=True)

            def last_used(n, units):
                pe.wait_ge(y_done, n * 4 + 4)
                pe.sem_inc(unit_used, units)

            def ffn(l, f, count):
                base = FFN_BASE[f]
                first_columns(l, base, count)
                columns(l, base + 1, 1, bank[1])

                def gate_up(j):
                    pe.wait_ge(silu_done, it(l, f, j) + 1)
                    columns(l, base + 3 * j + 2, 2, bank[0])
                    pe.wait_ge(hf_done, it(l, f, j) + 1)
                    columns(l, base + 3 * j + 3, 0, bank[1])

                def step(j, start):
                    gate_up(j)
                    pe.wait_ge(hlo_done, it(l, f, j) + 1)
                    pe.wait_ge(lo_ready, split(l, base + 3 * j + 4))
                    down(1, h_hi, h_lo, 0, (0, 1), start=start).then_inc(unit_used, 1)

                step(0, True)
                with pe.Fori(1, FP - 2) as j:
                    step(j, False)
                gate_up(FP - 2)
                pe.wait_ge(hlo_done, it(l, f, FP - 1))
                pe.wait_ge(lo_ready, split(l, base + FFN_UNITS - 2))
                for tb in range(2):
                    last = down(1, h_hi, h_lo, 0, (tb,))
                    if tb == 1:
                        last.then_inc(unit_used, 1)
                    if tb == 0:
                        pe.wait_ge(hlo_done, it(l, f, FP))
                        pe.wait_ge(lo_ready, split(l, base + FFN_UNITS - 1))
                    for half in range(2):
                        down(2, hl_hi, hl_lo, 0, (tb,), stop=True, halves=(half,)).then_inc(y_done, 1)
                last_used(phase(l, 2 * f), 1)

            def sb_scores(l, b):
                kb, heads = SB_BANKS[b]
                if b == 0:
                    pe.wait_ge(unit_evac, l * WIN_UNITS + 4)
                if b >= 2:
                    pe.wait_ge(w_done, l * 6 + (b - 1))
                m = 512 // len(heads)
                for i, h in enumerate(heads):
                    last = plain(Z[b % 2][:, i * m:(i + 1) * m], kpad[:, h, kb * P:(kb + 1) * P],
                                 qT[:, h // 2, T - m:T], start=i == 0)
                last.then_inc(z_done, 1)

            def sb_sums(l, b):
                kb, heads = SB_BANKS[b]
                z = Z[b % 2]
                pe.wait_ge(sp_lo_done, l * 6 + (b + 1))
                for part in (SP_HI, SP_LO):
                    last = plain(z[:, :], neg_r[:, 0, :], part[b % 3], stop=kb == 1 and part is SP_LO)
                if kb == 0:
                    later = SB_LATER[b]
                    c = SB_BANKS[later][1].index(heads[0]) * P
                    for part in (SP_HI, SP_LO):
                        last = plain(by_head(z, heads)[:, :, P:T], neg_r[:, 1, :],
                                     by_head(part[later % 3][:, c:c + T], heads), stop=part is SP_LO)
                last.then_inc(c_done, 1)

            def values(l, part, i):
                w = (stick_t, soft_t)[part]
                if part == 0:
                    pe.wait_ge(wm_done, l * 6 + 3 * (i + 1))
                    pe.wait_ge(unit_evac, l * WIN_UNITS + (9 + i))
                else:
                    pe.wait_ge(pt_done, l * 6 + 3 * (i + 1))
                    pe.wait_ge(unit_evac, l * WIN_UNITS + (11 + i))
                for h in range(4 * i, 4 * i + 4):
                    rows_of = slice((h % 2) * HD, (h % 2 + 1) * HD)
                    c = (h // 2 % 2) * T
                    d = slice(512 * part + h * HD, 512 * part + (h + 1) * HD)
                    plain(O[part][i][rows_of, c:c + T], v[:, 0, d], w[:, h, 0:T], start=True)
                    last = plain(O[part][i][rows_of, c + P:c + T], v[:, 1, d], w[:, h, T:T + P], stop=True)
                last.then_inc(o_done, 1)

            def head_means(l, part):
                for i in range(2):
                    pe.wait_ge(sq_done, l * 4 + (2 * part + i + 1))
                    plain(SS[i][:, :], head_mean, ez[:, i, :], start=True, stop=True).then_inc(ss_done, 1)

            def ca_scores(l, b):
                qb, heads = CA_BANKS[b]
                if b == 0:
                    pe.wait_ge(unit_evac, l * WIN_UNITS + 8)
                else:
                    pe.wait_ge(sa_done, l * 6 + b)
                m = 512 // len(heads)
                for i, h in enumerate(heads):
                    last = plain(bank[6][:, i * m:(i + 1) * m], qT[:, 4 + h // 2, qb * P:(qb + 1) * P],
                                 kpad[:, 8 + h, 0:m], start=True, stop=True)
                last.then_inc(t_done, 1)

            def ca_turn(l, b):
                pe.wait_ge(pn_done, l * 6 + (b + 1))
                if b > 0:
                    pe.wait_ge(pt_done, l * 6 + b)
                n = 512 // len(CA_BANKS[b][1]) // P
                for q in range(4):
                    c = (q % n) * P
                    last = nc.tensor.transpose(bank[7][:, q * P:(q + 1) * P],
                                               ca_view(soft_t, b)[:, q // n, c:c + P], ident)
                last.then_inc(x_done, 1)

            def w_in(l, a, halves=(0, 1)):
                if a >= 2 and halves[0] == 0:
                    pe.wait_ge(unit_evac, l * WIN_UNITS + (a - 1))
                f = rows if W_IN[a][0] == "v" else columns
                f(l, ATT0 + a, SLOT[ATT0 + a], bank[a % 2], halves)

            def attention(l):
                first_columns(l, ATT0, phase(l, 1))
                pe.wait_ge(band_turned, (l + 1) * 4)
                for a in range(1, 4):
                    w_in(l, a)
                w_in(l, 4, (0,))
                sb_scores(l, 0)
                w_in(l, 4, (1,))
                sb_scores(l, 1)
                for b in range(4):
                    w_in(l, 5 + b, (0,))
                    sb_sums(l, b)
                    if b == 3:
                        ca_scores(l, 0)
                    w_in(l, 5 + b, (1,))
                    sb_scores(l, b + 2)
                ca_scores(l, 1)
                w_in(l, 9, (0,))
                sb_sums(l, 4)
                ca_turn(l, 0)
                ca_scores(l, 2)
                w_in(l, 9, (1,))
                sb_sums(l, 5)
                ca_turn(l, 1)
                ca_scores(l, 3)
                w_in(l, 10, (0,))
                values(l, 0, 0)
                values(l, 0, 1)
                ca_turn(l, 2)
                ca_scores(l, 4)
                w_in(l, 10, (1,))
                head_means(l, 0)
                ca_turn(l, 3)
                ca_scores(l, 5)
                w_in(l, 11, (0,))
                ca_turn(l, 4)
                w_in(l, 11, (1,))
                ca_turn(l, 5)
                values(l, 1, 0)
                values(l, 1, 1)
                rels = [ATT0 + WIN_UNITS + i for i in range(WOUT_UNITS)]
                for i in range(2):
                    pe.wait_ge(mlo_done, l * 4 + (i + 1))
                    pe.wait_ge(lo_ready, split(l, rels[i]))
                    for tb in range(2):
                        for half in range(2):
                            if (i, tb, half) == (0, 0, 1):
                                pe.wait_ge(mix_done, l * 4 + 2)
                            last = down(SLOT[rels[i]], xT_hi, xT_lo, 2 * i, (tb,), start=i == 0, halves=(half,))
                        if tb == 1:
                            last.then_inc(unit_used, 1)
                        elif i == 0:
                            head_means(l, 1)
                for tb in range(2):
                    for i in (2, 3):
                        if tb == 0:
                            pe.wait_ge(mlo_done, l * 4 + (i + 1))
                            pe.wait_ge(lo_ready, split(l, rels[i]))
                        for half in range(2):
                            last = down(SLOT[rels[i]], xT_hi, xT_lo, 2 * i, (tb,), stop=i == 3, halves=(half,))
                            if i == 3:
                                last.then_inc(y_done, 1)
                last_used(phase(l, 1), 2)

            pe.wait_ge(consts, 12)
            with pe.Fori(0, DEPTH) as l:
                ffn(l, 0, phase(l, 0))
                turn_x(0, phase(l, 1))
                for i in range(3):
                    turn_band(l, i)
                turn_x(1, phase(l, 1))
                turn_band(l, 3)
                attention(l)
                turn_x(0, phase(l, 2))
                keep_warm(4)
                turn_x(1, phase(l, 2))
                ffn(l, 1, phase(l, 2))
                turn_x(0, phase(l, 3))
                keep_warm(4)
                turn_x(1, phase(l, 3))


_ARGS = ["x", "ffn1_w_gate", "ffn1_w_up", "ffn1_w_down", "ln1_g", "ln1_b", "w_in", "rel_bias", "sb_out_g",
         "ca_out_g", "w_out", "ln2_g", "ln2_b", "ffn2_w_gate", "ffn2_w_up", "ffn2_w_down", "ln3_g", "ln3_b"]


def column_units(w):
    k, n = w.shape
    return w.reshape(k // P, P, n // 256, 256).transpose(2, 1, 0, 3).reshape(n // 256, P, UW)


def row_units(w):
    return w.reshape(w.shape[0] // 256, 2, P, D).transpose(0, 2, 1, 3).reshape(-1, P, UW)


def weight_stream(ins):
    units = []
    for l in range(DEPTH):
        for f in ("ffn1", "ffn2"):
            g, u = (column_units(ins[f"{f}_w_{k}"][l]) for k in ("gate", "up"))
            d = row_units(ins[f"{f}_w_down"][l])
            units += [g[0], u[0]]
            for j in range(FP - 1):
                units += [g[j + 1], u[j + 1], d[j]]
            units.append(d[FP - 1])
            if f == "ffn1":
                w = column_units(ins["w_in"][l])
                units += [w[6 * part + 2 * "qkv".index(kind) + half] for kind, part, half in W_IN]
                units += list(row_units(ins["w_out"][l]))
    return np.stack(units)


def kernel(**inputs):
    import concourse.bacc as bacc
    from concourse.bass_utils import run_bass_kernel_spmd

    ins = {k: np.asarray(inputs[k]) for k in _ARGS}
    ln = np.stack([np.stack([ins[f"ln{i}_{k}"] for k in "gb"], 1) for i in (1, 2, 3)], 1)
    ln = ln.reshape(DEPTH * 3, 2, D)
    mix = np.concatenate([ins["sb_out_g"], ins["ca_out_g"]], 1).reshape(DEPTH, KC, P).transpose(0, 2, 1)
    flipped = ins["rel_bias"][:, :, ::-1]
    rel = np.concatenate([np.repeat(flipped[:, :, :1], P - 1, axis=2), flipped], 2)
    x = ins["x"].reshape(T, D)
    arrays = {
        "x": x,
        "xT": x.reshape(T, KC, P).transpose(2, 1, 0),
        "stream": weight_stream(ins),
        "ln_gb": ln,
        "mix_g": mix,
        "rel_band": rel,
    }
    arrays = {k: np.ascontiguousarray(a) for k, a in arrays.items()}
    nc = bacc.Bacc("TRN2", target_bir_lowering=False, num_devices=1)
    args = [nc.dram_tensor(k, a.shape, F32, kind="ExternalInput").ap() for k, a in arrays.items()]
    out = nc.dram_tensor("out", (T, D), F32, kind="ExternalOutput").ap()
    trunk(nc, *args, out)
    r = run_bass_kernel_spmd(nc, [arrays], core_ids=[0])
    return r.results[0]["out"].reshape(1, T, D)
```
